# Optimizing a Trainium2 kernel written in Bass

```python
import math
import jax, jax.numpy as jnp
from jax import lax
import numpy as np
import jax
import jax.numpy as jnp

D_MODEL = 1024
BATCH = 1
SEQ = 256
DEPTH = 2

BRANCH_WIDTH = 512
N_BRANCHES = 3
SWA_Q_HEADS = 8
SWA_KV_HEADS = 2
SWA_GROUP = SWA_Q_HEADS // SWA_KV_HEADS
SWA_HEAD_DIM = BRANCH_WIDTH // SWA_Q_HEADS
WINDOW = 128
N_BUCKETS = 32
MAX_DISTANCE = 128
CONV_CHANNELS = BRANCH_WIDTH
CONV_WIDTH = 31
MLA_HEADS = 8
MLA_Q_RANK = 256
MLA_KV_RANK = 128
MLA_NOPE_DIM = 64
MLA_ROPE_DIM = 32
MLA_V_DIM = BRANCH_WIDTH // MLA_HEADS
ROPE_THETA = 10000.0
Q_BLOCK = 128
D_FF = 4 * D_MODEL
EPS = 1e-6
NEG_INF = -1e30

IN_SPLIT_SIZES = (
    SWA_Q_HEADS * SWA_HEAD_DIM,
    SWA_KV_HEADS * SWA_HEAD_DIM,
    SWA_KV_HEADS * SWA_HEAD_DIM,
    2 * CONV_CHANNELS,
    MLA_Q_RANK,
    MLA_KV_RANK,
    MLA_ROPE_DIM,
    N_BRANCHES * D_MODEL,
)
IN_COLS = sum(IN_SPLIT_SIZES)
IN_SPLIT_POINTS = tuple(sum(IN_SPLIT_SIZES[: i + 1]) for i in range(len(IN_SPLIT_SIZES) - 1))


def rms_norm(x, g):
    xf = x.astype(jnp.float32)
    y = xf * lax.rsqrt(jnp.mean(xf * xf, axis=-1, keepdims=True) + EPS)
    return (y * g.astype(jnp.float32)).astype(x.dtype)

def layer_norm(x, g, b):
    xf = x.astype(jnp.float32)
    mu = jnp.mean(xf, axis=-1, keepdims=True)
    var = jnp.mean(jnp.square(xf - mu), axis=-1, keepdims=True)
    y = (xf - mu) * lax.rsqrt(var + EPS) * g.astype(jnp.float32) + b.astype(jnp.float32)
    return y.astype(x.dtype)

def t5_bucket(rel):
    n = jnp.maximum(rel, 0)
    max_exact = N_BUCKETS // 2
    nf = jnp.maximum(n, max_exact).astype(jnp.float32)
    large = max_exact + (jnp.log(nf / max_exact) / math.log(MAX_DISTANCE / max_exact)
                         * (N_BUCKETS - max_exact)).astype(jnp.int32)
    return jnp.where(n < max_exact, n, jnp.minimum(large, N_BUCKETS - 1))

def band_frames(t):
    b, s = t.shape[:2]
    blocks = t.reshape((b, s // WINDOW, WINDOW) + t.shape[2:])
    prev = jnp.concatenate([jnp.zeros_like(blocks[:, :1]), blocks[:, :-1]], axis=1)
    return jnp.concatenate([prev, blocks], axis=2)

def swa_bias_and_mask(positions, rel_bias):
    b, s = positions.shape
    nb = s // WINDOW
    pq = positions.reshape(b, nb, WINDOW)
    pk = band_frames(positions)
    bucket = t5_bucket(pq[..., :, None] - pk[..., None, :])
    bias = rel_bias[bucket].astype(jnp.float32).reshape(b, nb, WINDOW, 2 * WINDOW, SWA_KV_HEADS, SWA_GROUP)
    qi = WINDOW + jnp.arange(WINDOW)[:, None]
    ki = jnp.arange(2 * WINDOW)[None, :]
    in_band = (ki <= qi) & (qi - ki < WINDOW)
    has_prev = (jnp.arange(nb) > 0)[:, None, None] | (ki >= WINDOW)[None]
    mask = in_band[None] & has_prev
    return bias, mask[None, :, :, :, None, None]

def swa_attention(q, k, v, sinks, bias, mask):
    b, s = q.shape[:2]
    nb = s // WINDOW
    qb = q.reshape(b, nb, WINDOW, SWA_KV_HEADS, SWA_GROUP, SWA_HEAD_DIM)
    kk = band_frames(k.reshape(b, s, SWA_KV_HEADS, SWA_HEAD_DIM))
    vv = band_frames(v.reshape(b, s, SWA_KV_HEADS, SWA_HEAD_DIM))
    scores = jnp.einsum('bnqhgd,bnkhd->bnqkhg', qb, kk).astype(jnp.float32) * (SWA_HEAD_DIM ** -0.5) + bias
    scores = jnp.where(mask, scores, NEG_INF)
    sink = sinks.astype(jnp.float32).reshape(SWA_KV_HEADS, SWA_GROUP)
    m = jnp.maximum(scores.max(axis=3, keepdims=True), sink)
    p = jnp.exp(scores - m)
    p = p / (p.sum(axis=3, keepdims=True) + jnp.exp(sink - m))
    out = jnp.einsum('bnqkhg,bnkhd->bnqhgd', p.astype(vv.dtype), vv)
    return out.reshape(b, s, SWA_Q_HEADS * SWA_HEAD_DIM)

def conformer_conv(u_glu, w_dw, b_dw, g_ln, b_ln):
    a, gate = jnp.split(u_glu, 2, axis=-1)
    u = a * jax.nn.sigmoid(gate)
    u = lax.conv_general_dilated(u, w_dw, window_strides=(1,), padding=[(CONV_WIDTH - 1, 0)],
                                 dimension_numbers=('NWC', 'WIO', 'NWC'),
                                 feature_group_count=CONV_CHANNELS) + b_dw
    return jax.nn.silu(layer_norm(u, g_ln, b_ln))

def rope(x, positions):
    d = x.shape[-1]
    half = d // 2
    freqs = jnp.exp(-math.log(ROPE_THETA) * jnp.arange(half, dtype=jnp.float32) / half)
    ang = positions.astype(jnp.float32)[..., None] * freqs
    cos = jnp.cos(ang)[:, :, None, :]
    sin = jnp.sin(ang)[:, :, None, :]
    x1 = x[..., :half].astype(jnp.float32)
    x2 = x[..., half:].astype(jnp.float32)
    return jnp.concatenate([x1 * cos - x2 * sin, x2 * cos + x1 * sin], axis=-1).astype(x.dtype)

def mla_attention(cq, ckv, kpe_raw, positions, g_qn, w_uq, g_kvn, w_ukv):
    b, s = cq.shape[:2]
    q = (rms_norm(cq, g_qn) @ w_uq).reshape(b, s, MLA_HEADS, MLA_NOPE_DIM + MLA_ROPE_DIM)
    q_nope = q[..., :MLA_NOPE_DIM]
    q_pe = rope(q[..., MLA_NOPE_DIM:], positions)
    kv = (rms_norm(ckv, g_kvn) @ w_ukv).reshape(b, s, MLA_HEADS, MLA_NOPE_DIM + MLA_V_DIM)
    k_nope = kv[..., :MLA_NOPE_DIM]
    v = kv[..., MLA_NOPE_DIM:]
    k_pe = rope(kpe_raw[:, :, None, :], positions)[:, :, 0]
    scale = (MLA_NOPE_DIM + MLA_ROPE_DIM) ** -0.5
    nb = s // Q_BLOCK
    key_idx = jnp.arange(s)

    def to_blocks(t):
        return jnp.moveaxis(t.reshape((b, nb, Q_BLOCK) + t.shape[2:]), 1, 0)

    def attend_block(args):
        qn, qp, blk = args
        sc = (jnp.einsum('bqhd,bkhd->bhqk', qn, k_nope)
              + jnp.einsum('bqhd,bkd->bhqk', qp, k_pe)).astype(jnp.float32) * scale
        q_idx = blk * Q_BLOCK + jnp.arange(Q_BLOCK)
        sc = jnp.where(key_idx[None, :] <= q_idx[:, None], sc, NEG_INF)
        p = jax.nn.softmax(sc, axis=-1)
        return jnp.einsum('bhqk,bkhd->bqhd', p.astype(v.dtype), v)

    out = lax.map(attend_block, (to_blocks(q_nope), to_blocks(q_pe), jnp.arange(nb)))
    return jnp.moveaxis(out, 0, 1).reshape(b, s, MLA_HEADS * MLA_V_DIM)

def first_inputs(seed: int = 0) -> dict:
    key = jax.random.key(seed)
    ks = jax.random.split(key, 20)
    f32 = jnp.float32

    def nrm(k, shape, scale):
        return jax.random.normal(k, shape, f32) * scale

    def gain(k, shape):
        return 1.0 + 0.05 * jax.random.normal(k, shape, f32)

    return {
        "x": nrm(ks[0], (BATCH, SEQ, D_MODEL), 1.0),
        "positions": jnp.broadcast_to(jnp.arange(SEQ, dtype=jnp.int32), (BATCH, SEQ)),
        "rel_bias": nrm(ks[1], (N_BUCKETS, SWA_Q_HEADS), 0.5),
        "g_final": gain(ks[2], (D_MODEL,)),
        "g_mix": gain(ks[3], (DEPTH, D_MODEL)),
        "w_in": nrm(ks[4], (DEPTH, D_MODEL, IN_COLS), D_MODEL ** -0.5),
        "swa_sinks": nrm(ks[5], (DEPTH, SWA_Q_HEADS), 0.5),
        "g_q_norm": gain(ks[6], (DEPTH, MLA_Q_RANK)),
        "w_q_up": nrm(ks[7], (DEPTH, MLA_Q_RANK, MLA_HEADS * (MLA_NOPE_DIM + MLA_ROPE_DIM)), MLA_Q_RANK ** -0.5),
        "g_kv_norm": gain(ks[8], (DEPTH, MLA_KV_RANK)),
        "w_kv_up": nrm(ks[9], (DEPTH, MLA_KV_RANK, MLA_HEADS * (MLA_NOPE_DIM + MLA_V_DIM)), MLA_KV_RANK ** -0.5),
        "w_dw": nrm(ks[10], (DEPTH, CONV_WIDTH, 1, CONV_CHANNELS), CONV_WIDTH ** -0.5),
        "b_dw": nrm(ks[11], (DEPTH, CONV_CHANNELS), 0.02),
        "g_conv_ln": gain(ks[12], (DEPTH, CONV_CHANNELS)),
        "b_conv_ln": nrm(ks[13], (DEPTH, CONV_CHANNELS), 0.02),
        "w_branch": nrm(ks[14], (DEPTH, N_BRANCHES, BRANCH_WIDTH, D_MODEL), BRANCH_WIDTH ** -0.5),
        "w_out": nrm(ks[15], (DEPTH, D_MODEL, D_MODEL), D_MODEL ** -0.5),
        "g_mlp": gain(ks[16], (DEPTH, D_MODEL)),
        "w_up": nrm(ks[17], (DEPTH, D_MODEL, D_FF), D_MODEL ** -0.5),
        "w_down": nrm(ks[18], (DEPTH, D_FF, D_MODEL), D_FF ** -0.5),
    }

def first_block(x, positions, rel_bias, g_final, g_mix, w_in, swa_sinks, g_q_norm, w_q_up,
              g_kv_norm, w_kv_up, w_dw, b_dw, g_conv_ln, b_conv_ln, w_branch, w_out,
              g_mlp, w_up, w_down):
    b, s, _ = x.shape
    swa_bias, swa_mask = swa_bias_and_mask(positions, rel_bias)
    for l in range(DEPTH):
        h = rms_norm(x, g_mix[l])
        q_a, k_a, v_a, u_b, cq_c, ckv_c, kpe_c, gate_logits = jnp.split(h @ w_in[l], IN_SPLIT_POINTS, axis=-1)
        y_a = swa_attention(q_a, k_a, v_a, swa_sinks[l], swa_bias, swa_mask)
        y_b = conformer_conv(u_b, w_dw[l], b_dw[l], g_conv_ln[l], b_conv_ln[l])
        y_c = mla_attention(cq_c, ckv_c, kpe_c, positions, g_q_norm[l], w_q_up[l],
                            g_kv_norm[l], w_kv_up[l])
        branches = jnp.einsum('bsnc,ncd->bsnd', jnp.stack([y_a, y_b, y_c], axis=2), w_branch[l])
        gates = jax.nn.sigmoid(gate_logits.reshape(b, s, N_BRANCHES, D_MODEL))
        x = x + jnp.einsum('bsnd,bsnd->bsd', gates, branches) @ w_out[l]
        h = rms_norm(x, g_mlp[l])
        x = x + jnp.square(jax.nn.relu(h @ w_up[l])) @ w_down[l]
    return rms_norm(x, g_final)


DEPTH_2 = 1

GRID_W = 64
CTX_LEN = 256
H_RET = 4
RET_DK = 128
RET_DV = 128
RET_W = H_RET * RET_DV
H_GDN = 4
GDN_DK = 128
GDN_DV = 128
GDN_W = H_GDN * GDN_DV
SHORT_CONV = 3
CHUNK = 128
ROPE_BASE = 10000.0
N_STATE = 2 * RET_W + 2 * GDN_W + 4 * H_GDN
N_QUERY = 2 * RET_W + 2 * GDN_W + 2 * D_MODEL
N_IN = N_STATE + N_QUERY
N_EXPERTS = 64
TOP_K = 8
N_GROUPS = 8
TOPK_GROUPS = 4
D_EXPERT = 256
D_SHARED = 256
ROUTED_SCALE = 2.5
EXPERT_BLOCK = 128


def _rmsnorm(t, g):
    tf = t.astype(jnp.float32)
    y = tf * lax.rsqrt(jnp.mean(tf * tf, axis=-1, keepdims=True) + EPS)
    return (y * g.astype(jnp.float32)).astype(t.dtype)

def _l2norm(t):
    return t * lax.rsqrt(jnp.sum(t * t, axis=-1, keepdims=True) + EPS)

def _group_norm(t):
    tc = t - jnp.mean(t, axis=-1, keepdims=True)
    return tc * lax.rsqrt(jnp.mean(tc * tc, axis=-1, keepdims=True) + EPS)

def _head_rms(t):
    return t * lax.rsqrt(jnp.mean(t * t, axis=-1, keepdims=True) + EPS)

def _split_heads(t, n_heads):
    b, l, w = t.shape
    return t.reshape(b, l, n_heads, w // n_heads).transpose(0, 2, 1, 3)

def _merge_heads(t):
    b, h, l, d = t.shape
    return t.transpose(0, 2, 1, 3).reshape(b, l, h * d)

def _dwconv(t, w):
    return lax.conv_general_dilated(t, w[:, None, :].astype(t.dtype), (1,), 'SAME',
                                    dimension_numbers=('NWC', 'WIO', 'NWC'),
                                    feature_group_count=t.shape[-1])

def _modulation(cvec, w, b, n):
    m = jax.nn.silu(cvec) @ w[:, : n * D_MODEL] + b[: n * D_MODEL]
    return jnp.split(m, n, axis=-1)

def _axial_rope(n):
    rows = n // GRID_W
    pos_r = jnp.repeat(jnp.arange(rows, dtype=jnp.float32), GRID_W)
    pos_c = jnp.tile(jnp.arange(GRID_W, dtype=jnp.float32), rows)
    n_freq = RET_DK // 4
    inv = ROPE_BASE ** (-jnp.arange(n_freq, dtype=jnp.float32) / n_freq)
    ang = jnp.concatenate([pos_r[:, None] * inv, pos_c[:, None] * inv], axis=-1)
    return jnp.cos(ang), jnp.sin(ang)

def _apply_rope(t, cos, sin):
    half = RET_DK // 2
    t1, t2 = t[..., :half], t[..., half:]
    return jnp.concatenate([t1 * cos - t2 * sin, t1 * sin + t2 * cos], axis=-1)

def _retention_scan(q, k, v, log_g, s0):
    b, h, l, dk = k.shape
    n = l // CHUNK
    kc = k.reshape(b, h, n, CHUNK, dk)
    vc = v.reshape(b, h, n, CHUNK, -1)
    lg = log_g.astype(jnp.float32)[:, None]
    idx = jnp.arange(CHUNK, dtype=jnp.float32)
    kv = jnp.einsum('bhncd,hc,bhnce->bhnde', kc, jnp.exp(lg * (CHUNK - 1 - idx)), vc)
    chunk_decay = jnp.exp(lg[:, 0] * CHUNK)[None, :, None, None]

    def step(s, kv_n):
        return chunk_decay * s + kv_n, (None if q is None else s)

    s_fin, s_prev = lax.scan(step, s0, jnp.moveaxis(kv, 2, 0))
    if q is None:
        return s_fin
    qc = q.reshape(b, h, n, CHUNK, dk)
    dist = idx[:, None] - idx[None, :]
    dmat = jnp.where(dist >= 0, jnp.exp(lg[:, :, None] * jnp.maximum(dist, 0.0)), 0.0)
    scores = jnp.einsum('bhnid,bhnjd->bhnij', qc, kc) * dmat[None, :, None]
    o = jnp.einsum('bhnij,bhnje->bhnie', scores, vc)
    o = o + jnp.einsum('bhnid,nbhde->bhnie', qc, s_prev) * jnp.exp(lg * (idx + 1.0))[None, :, None, :, None]
    return o.reshape(b, h, l, -1), s_fin

def _gdn_scan(q, k, v, log_a, beta, s0):
    b, h, l, dk = k.shape
    dv = v.shape[-1]
    n = l // CHUNK
    kc = k.reshape(b, h, n, CHUNK, dk)
    vc = v.reshape(b, h, n, CHUNK, dv)
    bc = beta.reshape(b, h, n, CHUNK, 1)
    g = jnp.cumsum(log_a.reshape(b, h, n, CHUNK), axis=-1)
    idx = jnp.arange(CHUNK)
    strict = idx[:, None] > idx[None, :]
    rel = g[..., :, None] - g[..., None, :]
    a = jnp.einsum('bhnid,bhnjd->bhnij', kc, kc) * bc * jnp.where(strict, jnp.exp(jnp.where(strict, rel, 0.0)), 0.0)
    rhs = jnp.concatenate([bc * vc, bc * jnp.exp(g)[..., None] * kc], axis=-1)
    sol = lax.linalg.triangular_solve(a + jnp.eye(CHUNK, dtype=a.dtype), rhs,
                                      left_side=True, lower=True, unit_diagonal=True)
    u, wk = sol[..., :dv], sol[..., dv:]
    g_last = g[..., -1]
    k_tail = kc * jnp.exp(g_last[..., None] - g)[..., None]

    def step(s, inp):
        u_n, w_n, kt_n, gl_n = inp
        v_new = u_n - jnp.einsum('bhck,bhkv->bhcv', w_n, s)
        s_next = jnp.exp(gl_n)[..., None, None] * s + jnp.einsum('bhck,bhcv->bhkv', kt_n, v_new)
        return s_next, (None if q is None else (v_new, s))

    xs = tuple(jnp.moveaxis(t, 2, 0) for t in (u, wk, k_tail, g_last))
    s_fin, ys = lax.scan(step, s0, xs)
    if q is None:
        return s_fin
    v_new, s_prev = ys
    qc = q.reshape(b, h, n, CHUNK, dk)
    incl = idx[:, None] >= idx[None, :]
    qk = jnp.einsum('bhnid,bhnjd->bhnij', qc, kc) * jnp.where(incl, jnp.exp(jnp.where(incl, rel, 0.0)), 0.0)
    o = jnp.einsum('bhnij,nbhjv->bhniv', qk, v_new)
    o = o + jnp.einsum('bhnik,nbhkv->bhniv', qc * jnp.exp(g)[..., None], s_prev)
    return o.reshape(b, h, l, -1), s_fin

def _state_features(h, w_in_l, conv_l, a_log_l, dt_bias_l):
    p = h @ w_in_l[:, :N_STATE]
    rk = _split_heads(p[..., :RET_W].astype(jnp.float32), H_RET) * RET_DK ** -0.5
    rv = _split_heads(p[..., RET_W:2 * RET_W].astype(jnp.float32), H_RET)
    gkv = jax.nn.silu(_dwconv(p[..., 2 * RET_W:2 * RET_W + 2 * GDN_W], conv_l[:, GDN_W:])).astype(jnp.float32)
    gk = _l2norm(_split_heads(gkv[..., :GDN_W], H_GDN))
    gv = _split_heads(gkv[..., GDN_W:], H_GDN)
    b, l = h.shape[:2]
    gab = p[..., 2 * RET_W + 2 * GDN_W:].astype(jnp.float32).reshape(b, l, 2, 2, H_GDN).transpose(2, 3, 0, 4, 1)
    log_a = -jnp.exp(a_log_l.astype(jnp.float32))[:, None, :, None] * jax.nn.softplus(
        gab[0] + dt_bias_l.astype(jnp.float32)[:, None, :, None])
    beta = jax.nn.sigmoid(gab[1])
    return rk, rv, gk, gv, log_a, beta

def _query_features(h, w_in_l, conv_l):
    p = h @ w_in_l[:, N_STATE:]
    rq = _split_heads(p[..., :RET_W].astype(jnp.float32), H_RET)
    rg = p[..., RET_W:2 * RET_W]
    gq = jax.nn.silu(_dwconv(p[..., 2 * RET_W:2 * RET_W + GDN_W], conv_l[:, :GDN_W])).astype(jnp.float32)
    gq = _l2norm(_split_heads(gq, H_GDN)) * GDN_DK ** -0.5
    gz = p[..., 2 * RET_W + GDN_W:2 * RET_W + 2 * GDN_W]
    gates = jax.nn.sigmoid(p[..., 2 * RET_W + 2 * GDN_W:].astype(jnp.float32))
    return rq, rg, gq, gz, gates

def _recurrent_mixers(sf, rq, gq, init, ret_log_decay_l):
    rk, rv, gk, gv, log_a, beta = sf
    flip = lambda t: jnp.flip(t, axis=2)
    r_f = _retention_scan(rq, rk, rv, ret_log_decay_l[0], init[0])
    r_b = _retention_scan(None if rq is None else flip(rq), flip(rk), flip(rv), ret_log_decay_l[1], init[1])
    g_f = _gdn_scan(gq, gk, gv, log_a[0], beta[0], init[2])
    g_b = _gdn_scan(None if gq is None else flip(gq), flip(gk), flip(gv), flip(log_a[1]), flip(beta[1]), init[3])
    if rq is None:
        return (r_f, r_b, g_f, g_b)
    return r_f[0] + flip(r_b[0]), g_f[0] + flip(g_b[0]), (r_f[1], r_b[1], g_f[1], g_b[1])

def _mixer_out(ret_o, gdn_o, rg, gz, gates, ret_gn_w_l, gdn_norm_w_l, w_ret_out_l, w_gdn_out_l, w_o_l):
    dt = w_o_l.dtype
    ret_y = _merge_heads(_group_norm(ret_o)) * ret_gn_w_l.astype(jnp.float32) * jax.nn.silu(rg.astype(jnp.float32))
    gdn_y = _merge_heads(_head_rms(gdn_o)) * gdn_norm_w_l.astype(jnp.float32) * jax.nn.silu(gz.astype(jnp.float32))
    merged = (gates[..., :D_MODEL] * (ret_y.astype(dt) @ w_ret_out_l)
              + gates[..., D_MODEL:] * (gdn_y.astype(dt) @ w_gdn_out_l))
    return merged.astype(dt) @ w_o_l

def _moe(h, w_router_l, bias_l, w_gate_l, w_up_l, w_down_l, w_sh_gate_l, w_sh_up_l, w_sh_down_l):
    b, l, d = h.shape
    t = b * l
    xt = h.reshape(t, d)
    scores = jax.nn.sigmoid((xt @ w_router_l).astype(jnp.float32))
    biased = scores + bias_l.astype(jnp.float32)
    per_group = N_EXPERTS // N_GROUPS
    grp_score = lax.top_k(biased.reshape(t, N_GROUPS, per_group), 2)[0].sum(-1)
    grp_keep = jax.nn.one_hot(lax.top_k(grp_score, TOPK_GROUPS)[1], N_GROUPS, dtype=jnp.float32).sum(1) > 0
    cand = jnp.where(jnp.repeat(grp_keep, per_group, axis=1), biased, -jnp.inf)
    sel = lax.top_k(cand, TOP_K)[1]
    wts = jnp.take_along_axis(scores, sel, axis=1)
    wts = wts / jnp.sum(wts, axis=-1, keepdims=True) * ROUTED_SCALE
    n_assign = t * TOP_K
    flat_e = sel.reshape(-1)
    order = jnp.argsort(flat_e)
    e_sorted = flat_e[order]
    sizes = jnp.bincount(flat_e, length=N_EXPERTS).astype(jnp.int32)
    padded = (sizes + EXPERT_BLOCK - 1) // EXPERT_BLOCK * EXPERT_BLOCK
    pad_end = jnp.cumsum(padded)
    slot = (pad_end - padded)[e_sorted] + jnp.arange(n_assign, dtype=jnp.int32) - (jnp.cumsum(sizes) - sizes)[e_sorted]
    n_blocks = -(-n_assign // EXPERT_BLOCK) + N_EXPERTS
    n_slots = n_blocks * EXPERT_BLOCK
    slot_tok = jnp.full((n_slots,), t, jnp.int32).at[slot].set((order // TOP_K).astype(jnp.int32))
    slot_w = jnp.zeros((n_slots,), jnp.float32).at[slot].set(wts.reshape(-1)[order])
    block_e = jnp.minimum(jnp.searchsorted(pad_end, jnp.arange(n_blocks, dtype=jnp.int32) * EXPERT_BLOCK, side='right'),
                          N_EXPERTS - 1)
    xb = jnp.concatenate([xt, jnp.zeros((1, d), xt.dtype)])[slot_tok].reshape(n_blocks, EXPERT_BLOCK, d)

    def expert_block(args):
        xe, e = args
        return (jax.nn.silu(xe @ w_gate_l[e]) * (xe @ w_up_l[e])) @ w_down_l[e]

    yb = lax.map(expert_block, (xb, block_e)).reshape(n_slots, d)
    routed = jax.ops.segment_sum(yb * slot_w[:, None].astype(yb.dtype), slot_tok, num_segments=t + 1)[:t]
    shared = (jax.nn.silu(xt @ w_sh_gate_l) * (xt @ w_sh_up_l)) @ w_sh_down_l
    return (routed + shared).reshape(b, l, d)

def second_inputs(seed: int = 0) -> dict:
    key = jax.random.key(seed)
    ks = jax.random.split(key, 32)
    f32 = jnp.float32
    D = D_MODEL

    def nrm(k, shape, fan_in, scale=1.0):
        return jax.random.normal(k, shape, f32) * (scale * fan_in ** -0.5)

    def gain(k, shape):
        return 1.0 + 0.05 * jax.random.normal(k, shape, f32)

    base_decay = jnp.log1p(-jnp.power(2.0, -5.0 - jnp.arange(H_RET, dtype=f32)))
    dt = jnp.exp(jax.random.uniform(ks[12], (DEPTH_2, 2, H_GDN), f32, math.log(1e-3), math.log(1e-1)))
    return {
        'x': jax.random.normal(ks[0], (BATCH, SEQ, D), f32),
        'c': jax.random.normal(ks[1], (BATCH, D), f32),
        'ctx': jax.random.normal(ks[2], (BATCH, CTX_LEN, D), f32),
        'c_ctx': jax.random.normal(ks[3], (D,), f32),
        'w_mod': nrm(ks[4], (DEPTH_2, D, 6 * D), D, 0.3),
        'b_mod': 0.02 * jax.random.normal(ks[5], (DEPTH_2, 6 * D), f32),
        'norm_mix_pre': gain(ks[6], (DEPTH_2, D)),
        'norm_mix_post': gain(ks[7], (DEPTH_2, D)),
        'norm_ffn_pre': gain(ks[8], (DEPTH_2, D)),
        'norm_ffn_post': gain(ks[9], (DEPTH_2, D)),
        'w_in': nrm(ks[10], (DEPTH_2, D, N_IN), D),
        'gdn_conv': nrm(ks[11], (DEPTH_2, SHORT_CONV, 3 * GDN_W), SHORT_CONV),
        'ret_log_decay': base_decay * (1.0 + 0.05 * jax.random.normal(ks[13], (DEPTH_2, 2, H_RET), f32)),
        'gdn_a_log': jnp.log(jax.random.uniform(ks[14], (DEPTH_2, 2, H_GDN), f32, 1.0, 16.0)),
        'gdn_dt_bias': dt + jnp.log(-jnp.expm1(-dt)),
        'ret_gn_w': gain(ks[15], (DEPTH_2, RET_W)),
        'gdn_norm_w': gain(ks[16], (DEPTH_2, GDN_W)),
        'w_ret_out': nrm(ks[17], (DEPTH_2, RET_W, D), RET_W),
        'w_gdn_out': nrm(ks[18], (DEPTH_2, GDN_W, D), GDN_W),
        'w_o': nrm(ks[19], (DEPTH_2, D, D), D),
        'w_router': nrm(ks[20], (DEPTH_2, D, N_EXPERTS), D),
        'router_bias': 0.01 * jax.random.normal(ks[21], (DEPTH_2, N_EXPERTS), f32),
        'w_gate': nrm(ks[22], (DEPTH_2, N_EXPERTS, D, D_EXPERT), D),
        'w_up': nrm(ks[23], (DEPTH_2, N_EXPERTS, D, D_EXPERT), D),
        'w_down': nrm(ks[24], (DEPTH_2, N_EXPERTS, D_EXPERT, D), D_EXPERT),
        'w_sh_gate': nrm(ks[25], (DEPTH_2, D, D_SHARED), D),
        'w_sh_up': nrm(ks[26], (DEPTH_2, D, D_SHARED), D),
        'w_sh_down': nrm(ks[27], (DEPTH_2, D_SHARED, D), D_SHARED),
    }

def second_block(x, c, ctx, c_ctx, w_mod, b_mod, norm_mix_pre, norm_mix_post, norm_ffn_pre, norm_ffn_post,
              w_in, gdn_conv, ret_log_decay, gdn_a_log, gdn_dt_bias, ret_gn_w, gdn_norm_w,
              w_ret_out, w_gdn_out, w_o, w_router, router_bias, w_gate, w_up, w_down,
              w_sh_gate, w_sh_up, w_sh_down):
    b, n, _ = x.shape
    cos, sin = _axial_rope(n)
    zr = jnp.zeros((b, H_RET, RET_DK, RET_DV), jnp.float32)
    zg = jnp.zeros((b, H_GDN, GDN_DK, GDN_DV), jnp.float32)
    zero_state = (zr, zr, zg, zg)
    for i in range(DEPTH_2):
        last = i == DEPTH_2 - 1
        out_p = (ret_gn_w[i], gdn_norm_w[i], w_ret_out[i], w_gdn_out[i], w_o[i])
        moe_p = (w_router[i], router_bias[i], w_gate[i], w_up[i], w_down[i], w_sh_gate[i], w_sh_up[i], w_sh_down[i])
        sh1, sc1, g1, sh2, sc2, g2 = [m[:, None, :] for m in _modulation(c, w_mod[i], b_mod[i], 6)]
        cm = _modulation(c_ctx, w_mod[i], b_mod[i], 2 if last else 6)
        hc = _rmsnorm(ctx, norm_mix_pre[i]) * (1.0 + cm[1]) + cm[0]
        sf_c = _state_features(hc, w_in[i], gdn_conv[i], gdn_a_log[i], gdn_dt_bias[i])
        if last:
            init = _recurrent_mixers(sf_c, None, None, zero_state, ret_log_decay[i])
        else:
            rq_c, rg_c, gq_c, gz_c, gates_c = _query_features(hc, w_in[i], gdn_conv[i])
            ret_c, gdn_c, init = _recurrent_mixers(sf_c, rq_c, gq_c, zero_state, ret_log_decay[i])
            ctx = ctx + cm[2] * _rmsnorm(_mixer_out(ret_c, gdn_c, rg_c, gz_c, gates_c, *out_p), norm_mix_post[i])
            h2c = _rmsnorm(ctx, norm_ffn_pre[i]) * (1.0 + cm[4]) + cm[3]
            ctx = ctx + cm[5] * _rmsnorm(_moe(h2c, *moe_p), norm_ffn_post[i])
        hx = _rmsnorm(x, norm_mix_pre[i]) * (1.0 + sc1) + sh1
        rk, rv, gk, gv, log_a, beta = _state_features(hx, w_in[i], gdn_conv[i], gdn_a_log[i], gdn_dt_bias[i])
        rq, rg, gq, gz, gates = _query_features(hx, w_in[i], gdn_conv[i])
        sf_x = (_apply_rope(rk, cos, sin), rv, gk, gv, log_a, beta)
        ret_x, gdn_x, _ = _recurrent_mixers(sf_x, _apply_rope(rq, cos, sin), gq, init, ret_log_decay[i])
        x = x + g1 * _rmsnorm(_mixer_out(ret_x, gdn_x, rg, gz, gates, *out_p), norm_mix_post[i])
        h2 = _rmsnorm(x, norm_ffn_pre[i]) * (1.0 + sc2) + sh2
        x = x + g2 * _rmsnorm(_moe(h2, *moe_p), norm_ffn_post[i])
    return x


def setup_inputs(seed=0):
    out = dict(first_inputs(seed))
    for name, value in second_inputs(seed + 1).items():
        if name != "x":
            out[name + "_2"] = value
    return out


def reference(
    x, positions, rel_bias, g_final, g_mix, w_in, swa_sinks, g_q_norm, w_q_up, g_kv_norm,
    w_kv_up, w_dw, b_dw, g_conv_ln, b_conv_ln, w_branch, w_out, g_mlp, w_up, w_down, c_2, ctx_2,
    c_ctx_2, w_mod_2, b_mod_2, norm_mix_pre_2, norm_mix_post_2, norm_ffn_pre_2, norm_ffn_post_2,
    w_in_2, gdn_conv_2, ret_log_decay_2, gdn_a_log_2, gdn_dt_bias_2, ret_gn_w_2, gdn_norm_w_2,
    w_ret_out_2, w_gdn_out_2, w_o_2, w_router_2, router_bias_2, w_gate_2, w_up_2, w_down_2,
    w_sh_gate_2, w_sh_up_2, w_sh_down_2,
):
    x = first_block(
        x, positions, rel_bias, g_final, g_mix, w_in, swa_sinks, g_q_norm, w_q_up, g_kv_norm,
        w_kv_up, w_dw, b_dw, g_conv_ln, b_conv_ln, w_branch, w_out, g_mlp, w_up, w_down,
    )
    return second_block(
        x, c_2, ctx_2, c_ctx_2, w_mod_2, b_mod_2, norm_mix_pre_2, norm_mix_post_2,
        norm_ffn_pre_2, norm_ffn_post_2, w_in_2, gdn_conv_2, ret_log_decay_2, gdn_a_log_2,
        gdn_dt_bias_2, ret_gn_w_2, gdn_norm_w_2, w_ret_out_2, w_gdn_out_2, w_o_2, w_router_2,
        router_bias_2, w_gate_2, w_up_2, w_down_2, w_sh_gate_2, w_sh_up_2, w_sh_down_2,
    )


_drawn_inputs = setup_inputs


def setup_inputs(seed=0):
    import zlib

    import numpy as np

    out = dict(_drawn_inputs(seed))
    spreads = {}
    factors = {'swa_sinks': 5.902,
     'g_q_norm': 4.025,
     'g_kv_norm': 3.303,
     'b_conv_ln': 3.579,
     'norm_mix_post_2': 4.203,
     'norm_ffn_post_2': 6.246,
     'gdn_a_log_2': 2.812,
     'ret_gn_w_2': 4.008,
     'gdn_norm_w_2': 4.677}
    for name, (base, spread) in spreads.items():
        noise = np.random.default_rng([zlib.crc32(name.encode()), seed]).standard_normal(out[name].shape)
        drawn = base * np.exp(spread * noise) if base else spread * noise
        out[name] = jnp.asarray(drawn.astype(out[name].dtype))
    for name, factor in factors.items():
        out[name] = (out[name] * factor).astype(out[name].dtype)
    return out
```

```python
from contextlib import ExitStack

import numpy as np
import concourse.bass as bass
import concourse.mybir as mybir

ALU = mybir.AluOpType
ACT = mybir.ActivationFunctionType
AX = mybir.AxisListType
F32 = mybir.dt.float32
I32 = mybir.dt.int32
F32R = mybir.dt.float32r

P = 128
D = 1024
T = 256
KT = D // P
LAYERS = 2
EPS = 1e-6
NEG = -1e30

HEADS = 8
CONV_W = 31
N_BUCKETS = 32
FF_TILES = 32
SEG = ((0, 128), (128, 384))

CHUNK = 4096
SLOTS = 4
MOD_CHUNKS = 12
LAYER_CHUNKS = 32
MIX_CHUNKS = 16

RH = 4
C = 128
EXPERTS = 64
ROUTED_SCALE = 2.5

LP = {}
_at = 0
for _name, _n in (("g_mix", 8), ("g_mlp", 8), ("g_q", 2), ("g_kv", 1), ("w_dw", 4 * CONV_W), ("b_dw", 4),
                  ("g_ln", 4), ("b_ln", 4), ("sinks", 8)):
    LP[_name] = _at
    _at += _n
LP_COLS = _at

VP = {}
_at = 0
for _name, _n in (("g_final", 8), ("rel_bias", 256), ("c", 8), ("c_ctx", 8), ("b_mod", 48), ("mix_pre", 8),
                  ("mix_post", 8), ("ffn_pre", 8), ("ffn_post", 8), ("gdn_conv", 36), ("ret_gn", 4),
                  ("gdn_norm", 4), ("ret_decay", 8), ("a_log", 8), ("dt_bias", 8), ("router_bias", 64)):
    VP[_name] = _at
    _at += _n
VP_COLS = _at

CP = {}
_at = 0
for _name, _n in (("ident", 128), ("causal", 384), ("band", 384), ("thr", 32), ("rope_freq", 1), ("rope_sign", 1),
                  ("dist", 128), ("tri_f", 128), ("tri_b", 128), ("strict_f", 128), ("strict_b", 128),
                  ("level_f", 7 * 128), ("level_b", 7 * 128), ("row", 128), ("col", 4),
                  ("cos2", 128), ("sin2", 128)):
    CP[_name] = _at
    _at += _n
CP_COLS = _at
CP_FIRST = CP["dist"]

ARENA = 28160


def tables():
    t = np.zeros((P, CP_COLS), np.float32)

    def put(name, a):
        t[:a.shape[0], CP[name]:CP[name] + a.shape[1]] = a

    i = np.arange(P)
    put("ident", np.eye(P, dtype=np.float32))
    le = i[None, :] <= i[:, None]
    put("causal", np.where(np.concatenate([le, np.ones_like(le), le], 1), 0.0, NEG))
    put("band", np.where(np.concatenate([le, ~le, le], 1), 0.0, NEG))
    half = N_BUCKETS // 2
    thr = [b if b <= half else int(np.ceil(half * (128 / half) ** ((b - half) / half) - 1e-9))
           for b in range(N_BUCKETS)]
    put("thr", np.tile(np.array(thr, np.float32), (P, 1)))
    freq = np.exp(np.float32(-np.log(10000.0)) * np.arange(16, dtype=np.float32) / np.float32(16)).astype(np.float32)
    t[64:96, CP["rope_freq"]] = np.concatenate([freq, freq])
    t[64:96, CP["rope_sign"]] = np.repeat([-1.0, 1.0], 16)
    put("dist", (i[None, :] - i[:, None]).astype(np.float32))
    put("tri_f", (i[:, None] <= i[None, :]).astype(np.float32))
    put("tri_b", (i[:, None] >= i[None, :]).astype(np.float32))
    put("strict_f", (i[:, None] < i[None, :]).astype(np.float32))
    put("strict_b", (i[:, None] > i[None, :]).astype(np.float32))
    lf, lb = [], []
    for n in range(7):
        b = 1 << n
        pair = (i[:, None] // (2 * b)) == (i[None, :] // (2 * b))
        low = pair & ((i[:, None] // b) % 2 == 1) & ((i[None, :] // b) % 2 == 0)
        lf.append(low.T)
        lb.append(low)
    put("level_f", np.concatenate(lf, 1).astype(np.float32))
    put("level_b", np.concatenate(lb, 1).astype(np.float32))
    put("row", np.tile(i[None, :].astype(np.float32), (P, 1)))
    put("col", np.stack([i, P - 1 - i, i + 1, P - i], 1).astype(np.float32))
    n = np.arange(T)
    inv = (np.float32(10000.0) ** (-np.arange(32, dtype=np.float32) / np.float32(32))).astype(np.float32)
    ang = np.concatenate([(n // 64)[:, None].astype(np.float32) * inv, (n % 64)[:, None].astype(np.float32) * inv], 1)
    put("cos2", np.cos(ang).astype(np.float32).reshape(2, P, 64).transpose(1, 0, 2).reshape(P, 128))
    put("sin2", np.sin(ang).astype(np.float32).reshape(2, P, 64).transpose(1, 0, 2).reshape(P, 128))
    return t


PAIRS = (["x_norm", "q0", "q1", "kv", "cq", "ckv"] + [f"u{i}" for i in range(4)] + ["c_norm"]
         + [f"qup{i}" for i in range(4)] + [f"kup{i}" for i in range(4)] + ["vup0", "vup1"]
         + [f"gate{i}" for i in range(12)][:10] + ["conv_mean", "gate10", "conv_var", "gate11"]
         + [f"branch{i}" for i in range(12)] + [f"out{i}" for i in range(4)] + ["mlp_norm"]
         + [f"up{i}" for i in range(16)] + [f"down{i}" for i in range(4)])
PAIR_AT = {name: n for n, name in enumerate(PAIRS)}
assert len(PAIRS) % 2 == 0
BANK_PAIRS = len(PAIRS) // 2


def at(l, per_layer, n):
    return l * per_layer + n


def build(nc, stream, experts, params_once, params_layer, consts, positions, ctx_t, x_t, small, wt_rows, out):
    with ExitStack() as ctx:
        def sb(name, shape, dt=F32):
            return ctx.enter_context(nc.sbuf_tensor(name, shape, dt))

        def sem(name):
            return ctx.enter_context(nc.semaphore(name))

        ps = ctx.enter_context(nc.psum_tensor("ps", [P, 8, 512], F32))
        mem_at = -(-nc.sbuf_base // 32) * 32
        mem = sb("mem", [P, SLOTS * CHUNK + ARENA])
        ring = mem[:, 0:SLOTS * CHUNK].rearrange("p (s n) -> p s n", s=SLOTS)
        arena = mem[:, SLOTS * CHUNK:]
        def placed(name, at_, dims, dt=F32R):
            return nc.alloc_sbuf_tensor_at(name, [P, *dims], dt, offset=mem_at + 4 * at_)

        xT = sb("xT", [P, KT, T])
        cst = sb("cst", [P, CP_FIRST])
        vec = sb("vec", [P, VP_COLS])
        lay_all = sb("lay_all", [P, LAYERS, LP_COLS])
        lay = sb("lay", [P, LP_COLS])
        ones = sb("ones", [P, P])
        modT = sb("modT", [P, 48, 2])

        def carve(at_, *dims):
            n = int(np.prod(dims))
            v = arena[:, at_:at_ + n]
            if len(dims) == 1:
                return v
            names = "abc"[:len(dims)]
            return v.rearrange(f"p ({' '.join(names)}) -> p {' '.join(names)}", **dict(zip(names, dims)))

        gates = carve(0, 24, T)
        merged = carve(6144, KT, T)
        hidden = carve(0, FF_TILES, T)
        sq = carve(0, KT, T)
        qT = carve(8192, 4, T)
        kv = carve(9216, 2, T)
        cqT = carve(9728, 2, T)
        ckvT = carve(10240, 2, T)
        csq = carve(24568, 3, T)
        qcat = carve(10752, HEADS, T)
        kcat = carve(12800, HEADS, T)
        vm = carve(14848, 2, 512)
        yT = carve(15872, 12, T)
        upad = carve(18944, 4, T + CONV_W - 1)
        conv = carve(20088, 4, T)
        probs = carve(21112, 3, 384)
        pT = carve(22264, 2, 384)
        tanh_g = carve(23032, 2, T)
        relu = carve(23544, 2, 512)
        rot = carve(24568, KT * T // 2)
        stat = carve(25592, 2, T)
        hx = carve(26104, KT, T)
        bias = sb("bias", [P, HEADS, 384])
        rope_cs = sb("rope_cs", [P, 2, T])
        pos_i = sb("pos_i", [P, T + 2], I32)
        pos_f = carve(0, T + 2)
        dist = relu[:, 0, 0:384]
        reached = probs[:, 0, :]
        delta = sb("delta", [P, 256])
        turns = carve(512, 3, T)
        turns_i = carve(1280, T).bitcast(I32)
        half_w = sb("half_w", [P, 4 * CONV_W])
        nmax = sb("nmax", [P, 3, 4])
        esum = sb("esum", [P, 3, 4])
        csil = sb("csil", [P, KT, 2])

        def T_(name, n=None, start=0):
            return cst[:, CP[name] + start:CP[name] + start + n]

        def V_(name, k):
            return vec[:, VP[name] + k:VP[name] + k + 1]

        def L_(name, k):
            return lay[:, LP[name] + k:LP[name] + k + 1]

        s_load = sem("inputs_loaded")
        landed = [sem(f"chunk_landed_{s}") for s in range(SLOTS)]
        used = [sem(f"chunk_used_{s}") for s in range(SLOTS)]
        full = [sem(f"bank_full_{b}") for b in range(2)]
        free = [sem(f"bank_free_{b}") for b in range(2)]
        v_chain = sem("vector_step")
        a_chain = sem("scalar_step")
        s_ones = sem("ones_set")
        s_csil = sem("csil_ready")
        s_sil = sem("c_exp_ready")
        s_mod = sem("mod_full")
        s_modT = sem("mod_ready")
        s_ang = sem("angles_reduced")
        s_sin = sem("sin_ready")
        s_ld = sem("layer_start")
        s_sq = sem("squares_ready")
        s_var = sem("variance_ready")
        s_std = sem("deviation_ready")
        s_h = sem("h_ready")
        s_cn = sem("latents_normed")
        s_qk = sem("window_qk_ready")
        s_tg = sem("glu_tanh_ready")
        s_cq = sem("latents_copied")
        s_up = sem("latent_heads_copied")
        s_rot = sem("rotary_done")
        s_sf = sem("scores_full")
        s_sm = sem("scores_scaled")
        s_nm = sem("max_ready")
        s_ex = sem("exp_done")
        s_pn = sem("probs_ready")
        s_tf = sem("transposes_full")
        s_pt = sem("probs_turned")
        s_pv = sem("heads_done")
        s_y = sem("y_copied")
        s_cv = sem("conv_done")
        s_cc = sem("conv_centred")
        s_cl = sem("conv_scaled")
        s_yc = sem("y_conv_ready")
        s_g = sem("gates_ready")
        s_mg = sem("merged_ready")
        s_xo = sem("x_mixed")
        s_rl = sem("relu_ready")
        s_hd = sem("hidden_ready")
        s_hu = sem("relu_spent")
        s_end = sem("x_ready")
        s_out = sem("out_stored")

        class Step:

            def __init__(self, eng, s):
                self.eng, self.s, self.n = eng, s, 0

            def __call__(self, ins):
                self.n += 1
                ins.then_inc(self.s, 1)
                self.eng.wait_ge(self.s, self.n)

            def restart(self):
                self.eng.sem_clear(self.s)
                self.n = 0

        def bank_of(name):
            return PAIR_AT[name] % 2

        def pair(name):
            return ps[:, bank_of(name), :].rearrange("p (h t) -> p h t", h=2)

        def wait_free(eng, name, l):
            eng.wait_ge(free[bank_of(name)], at(l, BANK_PAIRS, PAIR_AT[name] // 2 + 1))

        def wait_read(eng, name, l):
            eng.wait_ge(free[bank_of(name)], at(l, BANK_PAIRS, PAIR_AT[name] // 2 + 2))

        def wait_full(eng, name, l):
            eng.wait_ge(full[bank_of(name)], at(l, BANK_PAIRS, PAIR_AT[name] // 2 + 1))

        def wait_chunk(pe, l, c):
            pe.wait_ge(landed[c % SLOTS], at(l, 16 * LAYER_CHUNKS // SLOTS, 16 * (MOD_CHUNKS // SLOTS + c // SLOTS + 1)))

        NCHUNK = MOD_CHUNKS + LAYERS * LAYER_CHUNKS + MIX_CHUNKS
        S_BANK, T_BANK, Y_BANK = 2, 4, 6

        c2 = carve(0, CP_COLS - CP_FIRST)
        hT = carve(2820, KT, 2 * T)
        vr = carve(6916, 4, RH, C)
        qr = carve(8964, 2, RH, C)
        qrT = carve(9988, RH, T)
        krT = carve(11012, RH, T)
        gpre = carve(12036, 8, 2, T + 2)
        gqpre = carve(12036 + 8 * 2 * (T + 2), 4, T + 2)
        gvT = carve(17196, RH, 2 * T)
        gkT = carve(19244, RH, 2 * T)
        gqT = carve(21292, RH, T)
        gkt = carve(22316, 4, RH, C)
        gvt = carve(24364, 4, RH, C)
        w_small = carve(26412, 640)
        sm = carve(27052, 1100)
        ctxT = carve(22316, KT, T)
        sq2 = carve(12036, KT, 2 * T)
        bflat = bias[:, :, :].rearrange("p h k -> p (h k)")
        kr = bflat[:, 0:2048].rearrange("p (t h d) -> p t h d", t=4, h=RH)
        o_ret = bflat[:, 2048:3072].rearrange("p (t h d) -> p t h d", t=2, h=RH)
        o_gdn = qr
        stat2 = carve(11012, 2 * T)
        buf = [[carve(12036 + 3072 * d + 512 * n, RH, C) for n in range(6)] for d in range(2)]
        AT, MT, X, XT, U, PT = range(6)
        state = [carve(18180 + 512 * d, RH, C) for d in range(2)]
        r_prev = [[carve(12036 + 512 * (2 * d + s), RH, C) for s in range(2)] for d in range(2)]
        r_ks = carve(14084, RH, C)
        r_qs = [carve(14596, RH, T), carve(15620, RH, T)]
        r_dm = carve(16644, RH, C)
        r_tmp = carve(17156, RH, C)
        rgT = carve(6916, 4, T)
        gzT = carve(7940, 4, T)
        gates2 = carve(22316, 16, T)
        ryT = carve(12036, 4, T)
        gyT = carve(13060, 4, T)
        merged2 = carve(14084, KT, T)
        mo = carve(16132, KT, T)
        oh = carve(18180, 2, RH, C)
        stat3 = carve(8964, 2 * T)
        h2T = carve(2820, KT, T)
        gu_mem = placed("gate_up_weights", 0, [2, CHUNK], F32)
        dn_mem = placed("down_weights", 8192, [2, 2048], F32)
        A0 = SLOTS * CHUNK
        gu_lo = placed("gate_up_rest", 0, [2, CHUNK])
        dn_lo = placed("down_rest", 8192, [2, 2048])
        h2_hi = placed("h2_rounded", 12288, [KT, T])
        h2_lo = placed("h2_rest", 12288 + KT * T, [KT, T])
        gu_hi = placed("gate_up_rounded", A0 + 12040, [2, CHUNK])
        dn_hi = placed("down_rounded", A0 + 20232, [2, 2048])
        hid_hi = placed("hidden_rounded", A0 + 24328, [2, 2, T])
        hid_lo = placed("hidden_rest", A0 + 25352, [2, 2, T])
        wrow = carve(4868, 2, T)
        silu_g = carve(5380, 2, 2, T)
        hid = carve(6404, 2, 2, T)
        wT_sb = carve(7428, T)
        zero = carve(7684, 512)
        ymoe = carve(12036, KT, T)
        sq3 = carve(14084, KT, T)
        stat4 = carve(8196, T)
        rw = carve(8452, 10, 2, 64)

        def C2(name, n=C, start=0):
            o = CP[name] - CP_FIRST + start
            return c2[:, o:o + n]

        la = sm[:, 0:32].rearrange("p (t c) -> p t c", t=4)
        beta = sm[:, 32:64].rearrange("p (t c) -> p t c", t=4)
        gcol = sm[:, 64:96].rearrange("p (t c) -> p t c", t=4)
        egcol = sm[:, 96:128].rearrange("p (t c) -> p t c", t=4)
        tmp_s = sm[:, 128:160].rearrange("p (t c) -> p t c", t=4)
        ealog = sm[:, 160:168]
        eglast = [sm[:, 168 + 4 * d:172 + 4 * d] for d in range(2)]
        glast = [sm[:, 176 + 4 * d:180 + 4 * d] for d in range(2)]
        etail = [sm[:, 184 + 4 * d:188 + 4 * d] for d in range(2)]
        kdec = sm[:, 192:200]
        cdec = sm[:, 200:208]
        gmix = sm[:, 208:224].rearrange("p (s k) -> p s k", s=2)
        gpost = sm[:, 224:232]
        gffn = sm[:, 232:240]
        gpost2 = sm[:, 240:248]
        r8 = sm[:, 248:256]
        r8b = sm[:, 256:264]
        ab = sm[:, 264:328].rearrange("p (t c) -> p t c", t=4)
        be = [sm[:, 328 + 4 * d:332 + 4 * d] for d in range(2)]
        ksc = sm[:, 336:340]
        tmp_b = sm[:, 340:372].rearrange("p (t c) -> p t c", t=4)

        STEPS = [(q, s) for q in range(2) for s in range(2)]

        def tile_of(q, s, d):
            return 2 * q + (s if d == 0 else 1 - s)

        F2 = ["fin", "norm"] + [f"rk{t}" for t in range(4)] + [f"rv{t}" for t in range(4)]
        F2 += [f"gk{h}" for h in range(4)] + [f"gv{h}" for h in range(4)] + ["gab"]
        F2 += ["rq2", "rq3", "gqA", "gqB"] + [f"l2k{h}" for h in range(4)] + ["l2qA", "l2qB"]
        F2 += ["krT2", "krT3", "qrT2", "qrT3"] + [f"gkt{t}" for t in range(4)] + [f"gvt{t}" for t in range(4)] + ["gcol"]
        for q, s in STEPS:
            F2 += [f"rkv{q}{s}{d}" for d in range(2)]
        F2 += ["oret2", "oret3"]
        for q, s in STEPS:
            for d in range(2):
                g = f"{q}{s}{d}"
                F2 += ["Gr" + g, "Br" + g, "KK" + g] + (["KQ" + g] if q else [])
            for n in range(7):
                F2 += [f"U{n}_{q}{s}{d}" for d in range(2)]
                for d in range(2):
                    F2 += ([f"XU{n}_{q}{s}{d}"] if n < 6 else []) + [f"UX{n}_{q}{s}{d}"]
            F2 += [f"w{q}{s}{d}" for d in range(2)] + [f"v{q}{s}{d}" for d in range(2)]
            if q:
                F2 += [f"Gq{q}{s}{d}" for d in range(2)] + [f"o{q}{s}{d}" for d in range(2)]
            F2 += [f"S{q}{s}{d}" for d in range(2)]
        F2 += [f"rg{i}" for i in range(2)] + [f"gz{i}" for i in range(2)] + [f"ga{i}" for i in range(8)]
        F2 += ["ryT0", "ryT1", "gyT0", "gyT1"]
        F2 += [f"wr{i}" for i in range(4)] + [f"wg{i}" for i in range(4)] + [f"wo{i}" for i in range(4)] + ["mnorm", "fnorm", "router", "wT"]
        F2_AT = {name: n for n, name in enumerate(F2)}
        assert len(F2_AT) == len(F2)
        full2 = [sem(f"result_full_{b}") for b in range(8)]
        free2 = [sem(f"result_free_{b}") for b in range(8)]
        events = {name: sem(name) for name in (
            "squares", "modulated", "unit_squares", "ret_rotated", "keys_normed",
            "decay_ready", "ret_keys_scaled", "ret_scores_wanted", "ret_scores", "ret_scores_decayed",
            "spread_0", "spread_1", "level_mask_0", "level_mask_1", "inverse_0", "inverse_1", "u_copied_0",
            "u_copied_1", "rhs_0", "rhs_1", "w_copied_0", "w_copied_1", "spread_q_0", "spread_q_1", "vnew_0",
            "vnew_1", "queries_0", "queries_1", "tail_0", "tail_1", "heads_normed", "branch_inputs", "merged2",
            "routing_ready", "gate_up_landed_0", "gate_up_landed_1", "silu_0",
            "silu_1", "hidden_0", "hidden_1", "gate_up_full_0", "gate_up_full_1", "down_landed_0",
            "down_landed_1", "down_done_0", "down_done_1", "y_sum", "scalar_step_2", "loads2",
            "mean_squares", "roots", "x_steps", "normed", "copied", "pads_clear", "conv_inputs",
            "convs", "decay_1", "decay_2",
            "ret_exps", "exponents", 
            "gcol_ready", "egcol_ready", "last_0", "last_1", "relative_0", "relative_1", "decays_0", "decays_1",
            "gq_exp_0", "gq_exp_1", "gates_ready_2", 
            "router_exp", "rows_ready_2", "rows_stored",
            "split_h2", "gate_up_rounded", "gate_up_rest", "down_rounded", "down_rest",
            "row_landed_0", "row_landed_1", "x_out", "vector_step_2",
        )}

        def E_(name):
            return events[name]

        def b2(name):
            return F2_AT[name] % 8

        def bank2(name, *dims):
            v = ps[:, b2(name), :]
            return v if not dims else v.rearrange("p (a b) -> p a b", a=dims[0])

        def room(pe, name):
            if F2_AT[name] >= 8:
                pe.wait_ge(free2[b2(name)], F2_AT[name] // 8)

        def got(eng, name):
            eng.wait_ge(full2[b2(name)], F2_AT[name] // 8 + 1)

        def read(eng, name):
            eng.sem_inc(free2[b2(name)], 1)

        def over(a, shape):
            return a.broadcast_to(shape)

        def heads_col(a, n=C):
            return a.rearrange("p (h o) -> p h o", o=1).broadcast_to([P, a.shape[1], n])

        def heads_row(a, h=RH):
            return a.rearrange("p (o n) -> p o n", o=1).broadcast_to([P, h, a.shape[1]])

        def second_tensor(pe):
            pend = [SLOTS - 1]
            chunk_at = [MOD_CHUNKS + LAYERS * LAYER_CHUNKS]
            ones_m = ones[:, :]

            def mul(o, lhs, rhs, start, stop, **kw):
                mm = nc.tensor.matmul(o, lhs, rhs, start=start, stop=stop, **kw)
                if pend and start and not stop:
                    mm.then_inc(used[pend.pop()], 1)
                return mm

            def take():
                c = chunk_at[0]
                chunk_at[0] += 1
                pe.wait_ge(landed[c % SLOTS], 16 * (c // SLOTS + 1))
                return ring[:, c % SLOTS, :]

            def spent():
                assert not pend
                pend.append((chunk_at[0] - 1) % SLOTS)

            def done(mm, name):
                mm.then_inc(full2[b2(name)], 1)

            def stats(name, src, nk, n, o=0):
                room(pe, name)
                for k in range(nk):
                    mm = mul(bank2(name)[:, o:o + n], ones_m, src(k), k == 0, k == nk - 1)
                done(mm, name)

            for s in range(2):
                for name in (f"gate_up_full_{s}", f"down_done_{s}", f"silu_{s}", f"hidden_{s}"):
                    pe.sem_inc(E_(name), 1)
            pe.wait_ge(E_("squares"), 1)
            stats("fin", lambda k: sq2[:, k, 0:T], KT, T)
            pe.wait_ge(E_("squares"), 2)
            stats("norm", lambda k: sq2[:, k, :], KT, 2 * T)
            pe.wait_ge(E_("modulated"), 1)
            for nm in ("rk", "rv"):
                w = take()
                for t in range(4):
                    room(pe, f"{nm}{t}")
                    for k in range(KT):
                        mm = mul(bank2(f"{nm}{t}"), hT[:, k, t * P:(t + 1) * P], w[:, k * 512:(k + 1) * 512], k == 0, k == KT - 1)
                    done(mm, f"{nm}{t}")
                spent()
            for nm in ("gk", "gv"):
                w = take()
                for h in range(4):
                    room(pe, f"{nm}{h}")
                    for k in range(KT):
                        mm = mul(bank2(f"{nm}{h}"), w[:, (h * KT + k) * P:(h * KT + k + 1) * P], hT[:, k, :], k == 0, k == KT - 1)
                    done(mm, f"{nm}{h}")
                spent()
            room(pe, "gab")
            for t in range(4):
                for k in range(KT):
                    mm = mul(bank2("gab")[:, 16 * t:16 * t + 16], hT[:, k, t * P:(t + 1) * P], w_small[:, 16 * k:16 * k + 16], k == 0, k == KT - 1)
            done(mm, "gab")
            w = take()
            for t in (2, 3):
                room(pe, f"rq{t}")
                for k in range(KT):
                    mm = mul(bank2(f"rq{t}"), hT[:, k, t * P:(t + 1) * P], w[:, k * 512:(k + 1) * 512], k == 0, k == KT - 1)
                done(mm, f"rq{t}")
            spent()

            def features(names, w, rhs, nk, o=0):
                for i, name in enumerate(names):
                    room(pe, name)
                    for j in range(2):
                        for k in range(nk):
                            a = o + ((2 * i + j) * nk + k) * P
                            mm = mul(bank2(name, 2)[:, j, :], w[:, a:a + P], rhs(k), k == 0, k == nk - 1)
                    done(mm, name)

            xh = lambda k: hT[:, k, T:2 * T]
            features(["gqA", "gqB"], take(), xh, KT)
            spent()
            for h in range(4):
                pe.wait_ge(E_("unit_squares"), h + 1)
                name = f"l2k{h}"
                room(pe, name)
                done(nc.tensor.matmul(bank2(name), ones_m, gkt[:, h, :, :].rearrange("p h d -> p (h d)"), start=True, stop=True), name)
            for i, nm in enumerate(("l2qA", "l2qB")):
                pe.wait_ge(E_("unit_squares"), i + 5)
                room(pe, nm)
                done(nc.tensor.matmul(bank2(nm), ones_m, gvt[:, i, :, :].rearrange("p h d -> p (h d)"), start=True, stop=True), nm)
            def turned(name, src):
                room(pe, name)
                for h in range(4):
                    mm = nc.tensor.transpose(bank2(name)[:, h * P:(h + 1) * P], src(h), T_("ident", P))
                done(mm, name)

            pe.wait_ge(E_("ret_rotated"), 1)
            for t in (2, 3):
                turned(f"krT{t}", lambda h: kr[:, t, h, :])
            for t in (2, 3):
                turned(f"qrT{t}", lambda h: qr[:, t - 2, h, :])
            pe.wait_ge(E_("keys_normed"), 1)
            for t in range(4):
                turned(f"gkt{t}", lambda h: gkT[:, h, t * P:(t + 1) * P])
            for t in range(4):
                turned(f"gvt{t}", lambda h: gvT[:, h, t * P:(t + 1) * P])
            pe.wait_ge(E_("decay_ready"), 1)
            room(pe, "gcol")
            for t in range(4):
                for d, tri in enumerate(("tri_f", "tri_b")):
                    mm = nc.tensor.matmul(bank2("gcol")[:, 8 * t + 4 * d:8 * t + 4 * d + 4], C2(tri), la[:, t, 4 * d:4 * d + 4], start=True, stop=True)
            done(mm, "gcol")

            n = 0
            for q, s in STEPS:
                for d in range(2):
                    t = tile_of(q, s, d)
                    n += 1
                    if (q, s) == (1, 1):
                        continue
                    pe.wait_ge(E_("ret_keys_scaled"), n)
                    name = f"rkv{q}{s}{d}"
                    room(pe, name)
                    for h in range(4):
                        mm = nc.tensor.matmul(bank2(name)[:, h * P:(h + 1) * P], r_ks[:, h, :], vr[:, t, h, :], start=True, stop=True)
                    done(mm, name)
            for d in range(2):
                name = f"rkv11{d}"
                room(pe, name)
                done(nc.tensor.matmul(bank2(name)[:, 0:2], ones_m, ones[:, 0:2], start=True, stop=True), name)
            for t in (2, 3):
                pe.wait_ge(E_("ret_scores_wanted"), t - 1)
                name = f"oret{t}"
                o = (t - 2) * P
                room(pe, name)
                for h in range(4):
                    mm = nc.tensor.matmul(bank2(name)[:, h * P:(h + 1) * P], krT[:, h, o:o + P], qrT[:, h, o:o + P], start=True, stop=True)
                mm.then_inc(E_("ret_scores"), 1)
                pe.wait_ge(E_("ret_scores_decayed"), t - 1)
                for h in range(4):
                    y = bank2(name)[:, h * P:(h + 1) * P]
                    nc.tensor.matmul(y, r_tmp[:, h, :], vr[:, t, h, :], start=True, stop=False)
                    nc.tensor.matmul(y, r_qs[0][:, h, o:o + P], r_prev[0][t - 2][:, h, :], start=False, stop=False)
                    mm = nc.tensor.matmul(y, r_qs[1][:, h, o:o + P], r_prev[1][t - 2][:, h, :], start=False, stop=True)
                done(mm, name)

            def heads4(name, lhs, rhs, more=None):
                room(pe, name)
                for h in range(4):
                    y = bank2(name)[:, h * P:(h + 1) * P]
                    mm = nc.tensor.matmul(y, lhs(h), rhs(h), start=True, stop=more is None)
                    if more is not None:
                        mm = nc.tensor.matmul(y, more[0](h), more[1](h), start=False, stop=True)
                done(mm, name)

            for i, (q, s) in enumerate(STEPS):
                for d in range(2):
                    t = tile_of(q, s, d)
                    g = f"{q}{s}{d}"
                    B = buf[d]
                    pe.wait_ge(E_(f"spread_{d}"), 2 * i + 1)
                    heads4("Gr" + g, lambda h: B[U][:, h, :], lambda h: C2("tri_f" if d == 0 else "tri_b"))
                    pe.wait_ge(E_(f"spread_{d}"), 2 * i + 2)
                    heads4("Br" + g, lambda h: B[X][:, h, :], lambda h: T_("ident", P))
                    kt = lambda h: gkT[:, h, t * P:(t + 1) * P]
                    heads4("KK" + g, kt, kt)
                    if q:
                        heads4("KQ" + g, kt, lambda h: gqT[:, h, (t - 2) * P:(t - 1) * P])
                for n in range(7):
                    for d in range(2):
                        B = buf[d]
                        pe.wait_ge(E_(f"level_mask_{d}"), 7 * i + n + 1)
                        pe.wait_ge(E_(f"inverse_{d}"), 7 * i + n + 1)
                        heads4(f"U{n}_{q}{s}{d}", lambda h: B[MT][:, h, :], lambda h: B[X][:, h, :])
                    for d in range(2):
                        B = buf[d]
                        pe.wait_ge(E_(f"u_copied_{d}"), 7 * i + n + 1)
                        if n < 6:
                            heads4(f"XU{n}_{q}{s}{d}", lambda h: B[XT][:, h, :], lambda h: B[U][:, h, :])
                        heads4(f"UX{n}_{q}{s}{d}", lambda h: B[U][:, h, :], lambda h: B[XT][:, h, :])
                for d in range(2):
                    B = buf[d]
                    pe.wait_ge(E_(f"rhs_{d}"), i + 1)
                    heads4(f"w{q}{s}{d}", lambda h: B[X][:, h, :], lambda h: B[XT][:, h, :])
                for d in range(2):
                    B = buf[d]
                    pe.wait_ge(E_(f"w_copied_{d}"), i + 1)
                    heads4(f"v{q}{s}{d}", lambda h: B[XT][:, h, :], lambda h: B[AT][:, h, :],
                           (lambda h: B[U][:, h, :], lambda h: state[d][:, h, :]))
                if q:
                    for d in range(2):
                        B = buf[d]
                        pe.wait_ge(E_(f"spread_q_{d}"), s + 1)
                        heads4(f"Gq{q}{s}{d}", lambda h: B[XT][:, h, :], lambda h: C2("tri_f" if d == 0 else "tri_b"))
                    for d in range(2):
                        B = buf[d]
                        pe.wait_ge(E_(f"vnew_{d}"), i + 1)
                        pe.wait_ge(E_(f"queries_{d}"), s + 1)
                        heads4(f"o{q}{s}{d}", lambda h: B[PT][:, h, :], lambda h: B[MT][:, h, :],
                               (lambda h: B[AT][:, h, :], lambda h: state[d][:, h, :]))
                for d in range(2):
                    B = buf[d]
                    pe.wait_ge(E_(f"vnew_{d}"), i + 1)
                    pe.wait_ge(E_(f"tail_{d}"), i + 1)
                    heads4(f"S{q}{s}{d}", lambda h: B[X][:, h, :], lambda h: B[MT][:, h, :])

            features(["rg0", "rg1"], take(), xh, KT)
            spent()
            features(["gz0", "gz1"], take(), xh, KT)
            spent()
            for i in range(4):
                features([f"ga{2 * i}", f"ga{2 * i + 1}"], take(), xh, KT)
                spent()
            for nm, src in (("ryT", o_ret), ("gyT", o_gdn)):
                pe.wait_ge(E_("heads_normed"), 1 if nm == "ryT" else 2)
                for t in range(2):
                    turned(f"{nm}{t}", lambda h: src[:, t, h, :])
            pe.wait_ge(E_("branch_inputs"), 1)
            features([f"wr{i}" for i in range(4)], take(), lambda k: ryT[:, k, :], 4)
            spent()
            pe.wait_ge(E_("branch_inputs"), 2)
            features([f"wg{i}" for i in range(4)], take(), lambda k: gyT[:, k, :], 4)
            spent()
            pe.wait_ge(E_("merged2"), 1)
            for i in range(2):
                features([f"wo{2 * i}", f"wo{2 * i + 1}"], take(), lambda k: merged2[:, k, :], KT)
                spent()
            pe.wait_ge(E_("squares"), 3)
            stats("mnorm", lambda k: gates2[:, k, :], KT, T)
            pe.wait_ge(E_("squares"), 4)
            stats("fnorm", lambda k: gates2[:, k, :], KT, T)
            pe.wait_ge(E_("modulated"), 2)
            room(pe, "router")
            for t in range(2):
                for k in range(KT):
                    mm = nc.tensor.matmul(bank2("router")[:, 64 * t:64 * t + 64], h2T[:, k, t * P:(t + 1) * P],
                                          w_small[:, 128 + 64 * k:192 + 64 * k], start=(k == 0), stop=(k == KT - 1))
            done(mm, "router")
            pe.wait_ge(E_("routing_ready"), 1)
            room(pe, "wT")
            for t in range(2):
                mm = nc.tensor.transpose(bank2("wT")[0:64, t * P:(t + 1) * P], rw[:, 2, t, :], T_("ident", P))
            done(mm, "wT")

            for b in range(8):
                pe.wait_ge(free2[b], (len(F2) - b + 7) // 8)
            for b in range(4):
                nc.tensor.matmul(ps[:, 4 + b, :], ones_m, zero, start=True, stop=True)

            pe.wait_ge(E_("split_h2"), 2)

            def three(o, w_hi, w_lo, x_hi, x_lo, start, stop, **kw):
                nc.tensor.matmul(o, w_hi, x_hi, start=start, stop=False, **kw)
                nc.tensor.matmul(o, w_hi, x_lo, start=False, stop=False, **kw)
                return nc.tensor.matmul(o, w_lo, x_hi, start=False, stop=stop, **kw)

            def gate_up(s, count):
                pe.wait_ge(E_("gate_up_rest"), count * 2 + s + 1)
                pe.wait_ge(E_(f"silu_{s}"), count + 1)
                pe.wait_ge(E_(f"hidden_{s}"), count + 1)
                for m in range(4):
                    for k in range(KT):
                        o = (m * KT + k) * P
                        mm = three(ps[:, 2 * s + m // 2, (m % 2) * T:(m % 2) * T + T], gu_hi[:, s, o:o + P], gu_lo[:, s, o:o + P],
                                   h2_hi[:, k, :], h2_lo[:, k, :], k == 0, k == KT - 1)
                mm.then_inc(E_(f"gate_up_full_{s}"), 1)

            def down(s, count):
                pe.wait_ge(E_("down_rest"), count * 2 + s + 1)
                pe.wait_ge(E_(f"hidden_{s}"), count + 2)
                for m in range(8):
                    for k in range(2):
                        o = (m * 2 + k) * P
                        mm = three(ps[:, 4 + m // 2, (m % 2) * T:(m % 2) * T + T], dn_hi[:, s, o:o + P], dn_lo[:, s, o:o + P],
                                   hid_hi[:, s, k, :], hid_lo[:, s, k, :], False, True, skip_group_check=True)
                mm.then_inc(E_(f"down_done_{s}"), 1)

            gate_up(0, 0)
            with pe.Fori(0, EXPERTS // 2) as j:
                gate_up(1, j)
                down(0, j)
                gate_up(0, j + 1)
                down(1, j)
            down(0, EXPERTS // 2)
            pe.wait_ge(E_("squares"), 5)
            for k in range(KT):
                mm = nc.tensor.matmul(ps[:, 0, 0:T], ones_m, sq3[:, k, :], start=(k == 0), stop=(k == KT - 1))
            mm.then_inc(E_("y_sum"), 1)

        def second_scalar(act):
            link = Step(act, E_("scalar_step_2"))
            A = nc.scalar.activation
            act.wait_ge(s_end, LAYERS)
            act.dma_start(c2, consts[:, CP_FIRST:]).then_inc(E_("loads2"), 16)
            act.dma_start(ctxT, ctx_t).then_inc(E_("loads2"), 16)
            act.dma_start(w_small, small).then_inc(E_("loads2"), 16)
            A(sq2[:, :, 0:T], xT[:, :, :], ACT.Square).then_inc(E_("squares"), 1)
            act.wait_ge(E_("mean_squares"), 1)
            A(stat2[:, 0:T], stat2[:, 0:T], ACT.Sqrt).then_inc(E_("roots"), 1)
            act.wait_ge(E_("x_steps"), 1)
            act.wait_ge(E_("loads2"), 48)
            A(sq2[:, :, 0:T], ctxT, ACT.Square)
            A(sq2[:, :, T:2 * T], xT[:, :, :], ACT.Square).then_inc(E_("squares"), 1)
            act.wait_ge(E_("mean_squares"), 2)
            A(stat2, stat2, ACT.Sqrt).then_inc(E_("roots"), 1)
            act.wait_ge(E_("normed"), 1)
            for q in range(2):
                for k in range(KT):
                    z = A(hT[:, k, q * T:(q + 1) * T], hT[:, k, q * T:(q + 1) * T], ACT.Identity,
                          bias=modT[:, k, 1 - q:2 - q], scale=gmix[:, q, k:k + 1])
            z.then_inc(E_("modulated"), 1)
            for t in range(4):
                got(act, f"rk{t}")
                link(A(kr[:, t, :, :].rearrange("p h d -> p (h d)"), bank2(f"rk{t}"), ACT.Copy, scale=float(C ** -0.5)))
                read(act, f"rk{t}")
            for t in range(4):
                got(act, f"rv{t}")
                link(nc.scalar.copy(vr[:, t, :, :].rearrange("p h d -> p (h d)"), bank2(f"rv{t}")))
                read(act, f"rv{t}")
            act.sem_inc(E_("copied"), 1)
            act.wait_ge(E_("pads_clear"), 1)
            for h in range(8):
                name = f"gk{h}" if h < 4 else f"gv{h - 4}"
                got(act, name)
                link(nc.scalar.copy(gpre[:, h, :, 1:T + 1], bank2(name, 2)))
                read(act, name)
                act.sem_inc(E_("conv_inputs"), 1)
            got(act, "gab")
            link(nc.scalar.copy(ab, ps[:, b2("gab"), 0:64].rearrange("p (t c) -> p t c", t=4)))
            read(act, "gab")
            act.sem_inc(E_("copied"), 1)
            for t in (2, 3):
                got(act, f"rq{t}")
                link(nc.scalar.copy(qr[:, t - 2, :, :].rearrange("p h d -> p (h d)"), bank2(f"rq{t}")))
                read(act, f"rq{t}")
            act.sem_inc(E_("copied"), 1)
            for i, nm in enumerate(("gqA", "gqB")):
                got(act, nm)
                link(nc.scalar.copy(gqpre[:, 2 * i:2 * i + 2, 1:T + 1], bank2(nm, 2)))
                read(act, nm)
                act.sem_inc(E_("conv_inputs"), 1)
            for h in range(4):
                act.wait_ge(E_("convs"), h + 1)
                link(A(gkT[:, h, :], gkT[:, h, :], ACT.Silu))
                A(gkt[:, h, :, :].rearrange("p h d -> p (h d)"), gkT[:, h, :], ACT.Square).then_inc(E_("unit_squares"), 1)
            for h in range(4):
                act.wait_ge(E_("convs"), h + 5)
                z = A(gvT[:, h, :], gvT[:, h, :], ACT.Silu)
            link(z)
            for i in range(2):
                act.wait_ge(E_("convs"), 2 * i + 10)
                link(A(gqT[:, 2 * i:2 * i + 2, :], gqT[:, 2 * i:2 * i + 2, :], ACT.Silu))
                A(gvt[:, i, :, :].rearrange("p (a h) d -> p a (h d)", a=2), gqT[:, 2 * i:2 * i + 2, :], ACT.Square).then_inc(E_("unit_squares"), 1)
            for h in range(6):
                act.wait_ge(E_("mean_squares"), h + 3)
                A(l2[h % 2], l2[h % 2], ACT.Sqrt).then_inc(E_("roots"), 1)
            act.wait_ge(E_("decay_1"), 1)
            A(tmp_s, tmp_s, ACT.Exp)
            A(beta, ab[:, :, 8:16], ACT.Exp, scale=-1.0)
            link(A(ealog, vec[:, VP["a_log"]:VP["a_log"] + 8], ACT.Exp))
            link(A(tmp_s, tmp_s, ACT.Ln, bias=1.0))
            act.sem_inc(E_("decay_2"), 1)
            for t in (2, 3):
                got(act, f"krT{t}")
                link(nc.scalar.copy(krT[:, :, (t - 2) * P:(t - 1) * P], bank2(f"krT{t}", 4)))
                read(act, f"krT{t}")
            for t in (2, 3):
                got(act, f"qrT{t}")
                link(nc.scalar.copy(qrT[:, :, (t - 2) * P:(t - 1) * P], bank2(f"qrT{t}", 4)))
                read(act, f"qrT{t}")
            act.sem_inc(E_("copied"), 1)
            for t in range(4):
                got(act, f"gkt{t}")
                link(nc.scalar.copy(gkt[:, t, :, :], bank2(f"gkt{t}", 4)))
                read(act, f"gkt{t}")
            for t in range(4):
                got(act, f"gvt{t}")
                link(nc.scalar.copy(gvt[:, t, :, :], bank2(f"gvt{t}", 4)))
                read(act, f"gvt{t}")
            act.sem_inc(E_("copied"), 1)
            for c in range(8):
                lg = V_("ret_decay", c)
                A(kdec[:, c:c + 1], C2("col", 1, 1 if c < 4 else 0), ACT.Exp, scale=lg)
                z = A(cdec[:, c:c + 1], lg, ACT.Exp, scale=float(C))
            z.then_inc(E_("ret_exps"), 1)
            act.wait_ge(E_("exponents"), 1)
            act.wait_ge(E_("copied"), 5)
            for c in range(8):
                lg = V_("ret_decay", c)
                for t in range(2):
                    z = A(r_qs[c // 4][:, c % 4, t * P:(t + 1) * P], rowb[c // 4], ACT.Exp, scale=lg)
            z.then_inc(E_("ret_exps"), 1)
            act.wait_ge(E_("exponents"), 2)
            for d in range(2):
                for h in range(4):
                    z = A((r_dm if d == 0 else r_tmp)[:, h, :], distm[d], ACT.Exp, scale=V_("ret_decay", 4 * d + h))
            z.then_inc(E_("ret_exps"), 1)

            act.wait_ge(E_("gcol_ready"), 1)
            link(A(egcol, gcol, ACT.Exp))
            act.sem_inc(E_("egcol_ready"), 1)
            for i, (q, s) in enumerate(STEPS):
                for d in range(2):
                    g = f"{q}{s}{d}"
                    B = buf[d]
                    act.wait_ge(E_(f"last_{d}"), i + 1)
                    A(eglast[d], glast[d], ACT.Exp)
                    link(A(etail[d], etail[d], ACT.Exp))
                    act.wait_ge(E_(f"relative_{d}"), i + 1)
                    link(A(B[PT], B[PT], ACT.Exp))
                    act.sem_inc(E_(f"decays_{d}"), 1)
                for n in range(7):
                    for d in range(2):
                        got(act, f"U{n}_{q}{s}{d}")
                        link(nc.scalar.copy(buf[d][U], bank2(f"U{n}_{q}{s}{d}", 4)))
                        read(act, f"U{n}_{q}{s}{d}")
                        act.sem_inc(E_(f"u_copied_{d}"), 1)
                for d in range(2):
                    got(act, f"w{q}{s}{d}")
                    link(A(buf[d][U], bank2(f"w{q}{s}{d}", 4), ACT.Copy, scale=-1.0))
                    read(act, f"w{q}{s}{d}")
                    act.sem_inc(E_(f"w_copied_{d}"), 1)
                for d in range(2):
                    got(act, f"v{q}{s}{d}")
                    link(nc.scalar.copy(buf[d][MT], bank2(f"v{q}{s}{d}", 4)))
                    read(act, f"v{q}{s}{d}")
                    act.sem_inc(E_(f"vnew_{d}"), 1)
                if q:
                    for d in range(2):
                        got(act, f"Gq{q}{s}{d}")
                        link(A(buf[d][AT], bank2(f"Gq{q}{s}{d}", 4), ACT.Exp))
                        read(act, f"Gq{q}{s}{d}")
                        act.sem_inc(E_(f"gq_exp_{d}"), 1)
            for i in range(2):
                got(act, f"rg{i}")
                link(A(rgT[:, 2 * i:2 * i + 2, :], bank2(f"rg{i}", 2), ACT.Silu))
                read(act, f"rg{i}")
            for i in range(2):
                got(act, f"gz{i}")
                link(A(gzT[:, 2 * i:2 * i + 2, :], bank2(f"gz{i}", 2), ACT.Silu))
                read(act, f"gz{i}")
            act.sem_inc(E_("gates_ready_2"), 1)
            for i in range(8):
                got(act, f"ga{i}")
                link(A(gates2[:, 2 * i:2 * i + 2, :], bank2(f"ga{i}", 2), ACT.Tanh, scale=0.5))
                read(act, f"ga{i}")
            act.sem_inc(E_("gates_ready_2"), 1)
            for n in range(2):
                act.wait_ge(E_("mean_squares"), n + 9)
                A(r8, r8, ACT.Sqrt).then_inc(E_("roots"), 1)
            act.wait_ge(E_("x_steps"), 2)
            A(gates2[:, 0:8, :], mo, ACT.Square).then_inc(E_("squares"), 1)
            act.wait_ge(E_("mean_squares"), 11)
            A(stat3[:, 0:T], stat3[:, 0:T], ACT.Sqrt).then_inc(E_("roots"), 1)
            act.wait_ge(E_("x_steps"), 3)
            A(gates2[:, 0:8, :], xT[:, :, :], ACT.Square).then_inc(E_("squares"), 1)
            act.wait_ge(E_("mean_squares"), 12)
            A(stat3[:, 0:T], stat3[:, 0:T], ACT.Sqrt).then_inc(E_("roots"), 1)
            act.wait_ge(E_("normed"), 2)
            for k in range(KT):
                z = A(h2T[:, k, :], h2T[:, k, :], ACT.Identity, bias=modT[:, 24 + k, 0:1], scale=gffn[:, k:k + 1])
            link(z)
            act.sem_inc(E_("modulated"), 1)
            nc.scalar.copy(h2_hi[:, :, :], h2T).then_inc(E_("split_h2"), 1)
            got(act, "router")
            link(A(rw[:, 0, :, :], ps[:, b2("router"), 0:P].rearrange("p (t e) -> p t e", t=2), ACT.Exp, scale=-1.0))
            read(act, "router")
            act.sem_inc(E_("router_exp"), 1)

            act.wait_ge(E_("rows_ready_2"), 1)
            act.dma_start(wt_rows, wT_sb[0:EXPERTS + 1, :]).then_inc(E_("rows_stored"), 16)

            def silu(s, count):
                act.wait_ge(E_(f"gate_up_full_{s}"), count + 2)
                act.wait_ge(E_(f"hidden_{s}"), count + 1)
                A(silu_g[:, s, :, :], ps[:, 2 * s, :].rearrange("p (a t) -> p a t", a=2), ACT.Silu).then_inc(E_(f"silu_{s}"), 1)

            def round_gu(s, count):
                act.wait_ge(E_(f"gate_up_landed_{s}"), (count + 1) * 16)
                for n in range(2):
                    o = slice(2048 * n, 2048 * n + 2048)
                    nc.scalar.copy(gu_hi[:, s, o], gu_mem[:, s, o]).then_inc(E_("gate_up_rounded"), 1)

            def round_dn(s, count):
                act.wait_ge(E_(f"down_landed_{s}"), (count + 1) * 16)
                nc.scalar.copy(dn_hi[:, s, :], dn_mem[:, s, :]).then_inc(E_("down_rounded"), 1)

            round_gu(0, 0)
            with act.Fori(0, EXPERTS // 2) as j:
                round_gu(1, j)
                round_dn(0, j)
                silu(0, j)
                round_gu(0, j + 1)
                round_dn(1, j)
                silu(1, j)
            round_dn(0, EXPERTS // 2)
            silu(0, EXPERTS // 2)
            act.wait_ge(E_("x_steps"), 4)
            A(sq3, ymoe, ACT.Square).then_inc(E_("squares"), 1)
            act.wait_ge(E_("mean_squares"), 13)
            A(stat4, stat4, ACT.Sqrt).then_inc(E_("roots"), 1)

        l2 = [carve(9988 + 512 * n, 2 * T) for n in range(2)]
        rowb = [carve(17668 + 128 * n, C) for n in range(2)]
        distm = [carve(17924 + 128 * n, C) for n in range(2)]

        def sync_tail(sp):
            for s in range(SLOTS):
                sp.wait_ge(used[s], NCHUNK // SLOTS + 1)
            sp.wait_ge(E_("rows_stored"), 16)

            def expert(s, e, count):
                sp.wait_ge(E_(f"gate_up_full_{s}"), count + 1)
                sp.dma_start(gu_mem[:, s, :], experts[bass.ds(e, 1), :, 0:CHUNK].rearrange("a p n -> p (a n)")).then_inc(E_(f"gate_up_landed_{s}"), 16)
                sp.wait_ge(E_(f"hidden_{s}"), count + 1)
                sp.dma_start(wrow[:, s, :], wt_rows[bass.ds(e, 1), :].broadcast_to([P, T])).then_inc(E_(f"row_landed_{s}"), 16)
                sp.wait_ge(E_(f"down_done_{s}"), count + 1)
                sp.dma_start(dn_mem[:, s, :], experts[bass.ds(e, 1), :, CHUNK:].rearrange("a p n -> p (a n)")).then_inc(E_(f"down_landed_{s}"), 16)

            with sp.Fori(0, EXPERTS // 2) as j:
                expert(0, j * 2, j)
                expert(1, j * 2 + 1, j)
            expert(0, EXPERTS, EXPERTS // 2)
            sp.wait_ge(E_("x_out"), 1)
            sp.dma_start(out, xT[:, :, :]).then_inc(s_out, 16)
            sp.wait_ge(s_out, 16)

        def second_vector(dve):
            link = Step(dve, E_("vector_step_2"))
            tt, ts, stt = nc.vector.tensor_tensor, nc.vector.tensor_scalar, nc.vector.scalar_tensor_tensor
            cp, red = nc.vector.tensor_copy, nc.vector.tensor_reduce

            def inv(a, src, n):
                link(ts(a, src, 1.0 / n, EPS, ALU.mult, ALU.add))

            got(dve, "fin")
            inv(stat2[:, 0:T], bank2("fin")[:, 0:T], D)
            read(dve, "fin")
            nc.vector.reciprocal(stat2[:, 0:T], stat2[:, 0:T]).then_inc(E_("mean_squares"), 1)
            dve.wait_ge(E_("roots"), 1)
            for k in range(KT):
                z = stt(xT[:, k, :], xT[:, k, :], V_("g_final", k), stat2[:, 0:T], ALU.mult, ALU.mult)
            link(z)
            dve.sem_inc(E_("x_steps"), 1)
            dve.wait_ge(E_("loads2"), 48)
            for q in range(2):
                tt(gmix[:, q, :], vec[:, VP["mix_pre"]:VP["mix_pre"] + 8], modT[:, 8:16, 1 - q], ALU.mult)
            tt(gpost, vec[:, VP["mix_post"]:VP["mix_post"] + 8], modT[:, 16:24, 0], ALU.mult)
            tt(gffn, vec[:, VP["ffn_pre"]:VP["ffn_pre"] + 8], modT[:, 32:40, 0], ALU.mult)
            link(tt(gpost2, vec[:, VP["ffn_post"]:VP["ffn_post"] + 8], modT[:, 40:48, 0], ALU.mult))
            got(dve, "norm")
            inv(stat2, bank2("norm"), D)
            read(dve, "norm")
            nc.vector.reciprocal(stat2, stat2).then_inc(E_("mean_squares"), 1)
            dve.wait_ge(E_("roots"), 2)
            tt(hT[:, :, 0:T], ctxT, heads_row(stat2[:, 0:T], KT), ALU.mult)
            link(tt(hT[:, :, T:2 * T], xT[:, :, :], heads_row(stat2[:, T:2 * T], KT), ALU.mult))
            dve.sem_inc(E_("normed"), 1)
            for o in (0, T + 1):
                nc.vector.memset(gpre[:, :, :, o:o + 1], 0.0)
                z = nc.vector.memset(gqpre[:, :, o:o + 1], 0.0)
            link(z)
            dve.sem_inc(E_("pads_clear"), 1)
            cw = VP["gdn_conv"]

            def conv3(dst, src, tap):
                w = [vec[:, cw + 3 * tap + i:cw + 3 * tap + i + 1] for i in range(3)]
                link(ts(dst, src(0), w[0], None, ALU.mult))
                link(stt(dst, src(1), w[1], dst, ALU.mult, ALU.add))
                link(stt(dst, src(2), w[2], dst, ALU.mult, ALU.add))
                dve.sem_inc(E_("convs"), 1)

            for h in range(8):
                dve.wait_ge(E_("conv_inputs"), h + 1)
                dst = (gkT if h < 4 else gvT)[:, h % 4, :].rearrange("p (q t) -> p q t", q=2)
                conv3(dst, lambda i: gpre[:, h, :, i:i + T], 4 + h)
            dve.wait_ge(E_("copied"), 2)
            dt_ = vec[:, VP["dt_bias"]:VP["dt_bias"] + 8].rearrange("p (o c) -> p o c", o=1).broadcast_to([P, 4, 8])
            link(tt(la, ab[:, :, 0:8], dt_, ALU.add))
            link(ts(tmp_s, la, -1.0, None, ALU.mult))
            link(tt(tmp_s, tmp_s, la, ALU.min))
            link(ts(la, la, 0.0, None, ALU.max))
            dve.sem_inc(E_("decay_1"), 1)
            for h in range(4):
                dve.wait_ge(E_("conv_inputs"), 9 + h // 2)
                conv3(gqT[:, h, :], lambda i: gqpre[:, h, i:i + T], h)
            for h in range(6):
                name = f"l2k{h}" if h < 4 else ("l2qA", "l2qB")[h - 4]
                got(dve, name)
                link(ts(l2[h % 2], bank2(name), EPS, None, ALU.add))
                read(dve, name)
                nc.vector.reciprocal(l2[h % 2], l2[h % 2]).then_inc(E_("mean_squares"), 1)
                dve.wait_ge(E_("roots"), h + 3)
                if h < 4:
                    link(tt(gkT[:, h, :], gkT[:, h, :], l2[h % 2], ALU.mult))
                else:
                    a = gqT[:, 2 * (h - 4):2 * (h - 4) + 2, :]
                    link(stt(a, l2[h % 2].rearrange("p (a t) -> p a t", a=2), float(C ** -0.5), a, ALU.mult, ALU.mult))
            dve.sem_inc(E_("keys_normed"), 1)
            dve.wait_ge(E_("decay_2"), 1)
            link(tt(la, la, tmp_s, ALU.add))
            ea = ealog.rearrange("p (o c) -> p o c", o=1).broadcast_to([P, 4, 8])
            link(ts(la, la, -1.0, None, ALU.mult))
            link(tt(la, la, ea, ALU.mult))
            link(ts(beta, beta, 1.0, None, ALU.add))
            link(nc.vector.reciprocal(beta, beta))
            dve.sem_inc(E_("decay_ready"), 1)
            dve.wait_ge(E_("copied"), 1)
            dve.wait_ge(E_("copied"), 3)
            s1, s2 = (l2[n][:, 0:256].rearrange("p (h d) -> p h d", h=4) for n in range(2))
            for t in range(2):
                cos = heads_row(C2("cos2", 64, 64 * t))
                sin = heads_row(C2("sin2", 64, 64 * t))
                for a in (kr[:, 2 + t, :, :], qr[:, t, :, :]):
                    a1, a2 = a[:, :, 0:64], a[:, :, 64:128]
                    tt(s1, a1, sin, ALU.mult)
                    link(tt(s2, a2, sin, ALU.mult))
                    tt(a1, a1, cos, ALU.mult)
                    link(tt(a2, a2, cos, ALU.mult))
                    tt(a1, a1, s2, ALU.subtract)
                    link(tt(a2, a2, s1, ALU.add))
            dve.sem_inc(E_("ret_rotated"), 1)
            got(dve, "gcol")
            link(cp(gcol, ps[:, b2("gcol"), 0:32].rearrange("p (t c) -> p t c", t=4)))
            read(dve, "gcol")
            dve.sem_inc(E_("gcol_ready"), 1)

            dve.wait_ge(E_("copied"), 5)
            ts(rowb[0], C2("row"), 1.0, None, ALU.add)
            link(ts(rowb[1], C2("row"), -1.0, float(C), ALU.mult, ALU.add))
            dve.sem_inc(E_("exponents"), 1)
            ts(distm[0], C2("dist"), 0.0, None, ALU.max)
            link(ts(distm[1], C2("dist"), -1.0, 0.0, ALU.mult, ALU.max))
            dve.sem_inc(E_("exponents"), 1)
            dve.wait_ge(E_("ret_exps"), 1)
            prev = [None, None]
            for q, s in STEPS[:3]:
                for d in range(2):
                    t = tile_of(q, s, d)
                    name = f"rkv{q}{s}{d}"
                    link(tt(r_ks, kr[:, t, :, :], heads_col(kdec[:, 4 * d:4 * d + 4]), ALU.mult))
                    dve.sem_inc(E_("ret_keys_scaled"), 1)
                    got(dve, name)
                    dst = r_prev[d][d if q == 0 else 1 - d]
                    for h in range(4):
                        kvh = bank2(name)[:, h * P:(h + 1) * P]
                        if prev[d] is None:
                            z = cp(dst[:, h, :], kvh)
                        else:
                            z = stt(dst[:, h, :], prev[d][:, h, :], cdec[:, 4 * d + h:4 * d + h + 1], kvh, ALU.mult, ALU.add)
                    link(z)
                    prev[d] = dst
                    read(dve, name)
            for d in range(2):
                got(dve, f"rkv11{d}")
                read(dve, f"rkv11{d}")
            dve.wait_ge(E_("ret_exps"), 2)
            dve.wait_ge(E_("copied"), 4)
            for d in range(2):
                z = tt(r_qs[d], r_qs[d], qrT, ALU.mult)
            link(z)
            dve.wait_ge(E_("ret_exps"), 3)
            tt(r_dm, r_dm, heads_row(C2("tri_f")), ALU.mult)
            link(tt(r_tmp, r_tmp, heads_row(C2("tri_b")), ALU.mult))
            link(tt(r_dm, r_dm, r_tmp, ALU.add))
            dve.sem_inc(E_("ret_scores_wanted"), 2)
            for t in (2, 3):
                name = f"oret{t}"
                dve.wait_ge(E_("ret_scores"), t - 1)
                link(tt(r_tmp, r_dm, bank2(name, 4), ALU.mult))
                dve.sem_inc(E_("ret_scores_decayed"), 1)
                got(dve, name)
                link(cp(o_ret[:, t - 2, :, :], bank2(name, 4)))
                read(dve, name)

            dve.wait_ge(E_("egcol_ready"), 1)
            for d in range(2):
                z = nc.vector.memset(state[d], 0.0)
            link(z)
            for i, (q, s) in enumerate(STEPS):
                for d in range(2):
                    t = tile_of(q, s, d)
                    e = slice(4 * d, 4 * d + 4)
                    link(cp(buf[d][U], heads_col(la[:, t, e])))
                    dve.sem_inc(E_(f"spread_{d}"), 1)
                    link(cp(buf[d][X], heads_col(beta[:, t, e])))
                    dve.sem_inc(E_(f"spread_{d}"), 1)
                    tt(be[d], beta[:, t, e], egcol[:, t, e], ALU.mult)
                for d in range(2):
                    t = tile_of(q, s, d)
                    e = slice(4 * d, 4 * d + 4)
                    g = f"{q}{s}{d}"
                    B = buf[d]
                    tri = heads_row(C2("tri_f" if d == 0 else "tri_b"))
                    got(dve, "Gr" + g)
                    Gr = bank2("Gr" + g, 4)
                    lastcol = Gr[:, :, (C - 1) if d == 0 else 0]
                    cp(glast[d], lastcol)
                    tt(etail[d], lastcol, gcol[:, t, e], ALU.subtract)
                    link(tt(B[PT], Gr, heads_col(gcol[:, t, e]), ALU.subtract))
                    read(dve, "Gr" + g)
                    dve.sem_inc(E_(f"last_{d}"), 1)
                    link(tt(B[PT], B[PT], tri, ALU.mult))
                    dve.sem_inc(E_(f"relative_{d}"), 1)
                for d in range(2):
                    g = f"{q}{s}{d}"
                    B = buf[d]
                    tri = heads_row(C2("tri_f" if d == 0 else "tri_b"))
                    strict = heads_row(C2("strict_f" if d == 0 else "strict_b"))
                    dve.wait_ge(E_(f"decays_{d}"), i + 1)
                    link(tt(B[PT], B[PT], tri, ALU.mult))
                    link(tt(B[AT], B[PT], strict, ALU.mult))
                    got(dve, "KK" + g)
                    link(tt(B[AT], B[AT], bank2("KK" + g, 4), ALU.mult))
                    read(dve, "KK" + g)
                    got(dve, "Br" + g)
                    link(tt(B[AT], B[AT], bank2("Br" + g, 4), ALU.mult))
                    read(dve, "Br" + g)
                    lev = "level_f" if d == 0 else "level_b"
                    tt(B[MT], B[AT], heads_row(C2(lev)), ALU.mult)
                    cp(B[X], heads_row(T_("ident", P)))
                    link(cp(B[XT], heads_row(T_("ident", P))))
                    dve.sem_inc(E_(f"level_mask_{d}"), 1)
                    dve.sem_inc(E_(f"inverse_{d}"), 1)
                    if q:
                        got(dve, "KQ" + g)
                        link(tt(B[PT], B[PT], bank2("KQ" + g, 4), ALU.mult))
                        read(dve, "KQ" + g)
                for n in range(7):
                    for d in range(2):
                        B = buf[d]
                        g = f"{n}_{q}{s}{d}"
                        if n < 6:
                            lev = "level_f" if d == 0 else "level_b"
                            got(dve, "U" + g)
                            link(tt(B[MT], B[AT], heads_row(C2(lev, C, C * (n + 1))), ALU.mult))
                            dve.sem_inc(E_(f"level_mask_{d}"), 1)
                    for d in range(2):
                        B = buf[d]
                        g = f"{n}_{q}{s}{d}"
                        if n < 6:
                            got(dve, "XU" + g)
                            link(tt(B[X], B[X], bank2("XU" + g, 4), ALU.subtract))
                            read(dve, "XU" + g)
                        got(dve, "UX" + g)
                        link(tt(B[XT], B[XT], bank2("UX" + g, 4), ALU.subtract))
                        read(dve, "UX" + g)
                        if n < 6:
                            dve.sem_inc(E_(f"inverse_{d}"), 1)
                for d in range(2):
                    t = tile_of(q, s, d)
                    e = slice(4 * d, 4 * d + 4)
                    B = buf[d]
                    tt(B[AT], gvt[:, t, :, :], heads_col(beta[:, t, e]), ALU.mult)
                    link(tt(B[X], gkt[:, t, :, :], heads_col(be[d]), ALU.mult))
                    dve.sem_inc(E_(f"rhs_{d}"), 1)
                for d in range(2):
                    t = tile_of(q, s, d)
                    got(dve, f"w{q}{s}{d}")
                    link(tt(buf[d][X], gkt[:, t, :, :], heads_col(etail[d]), ALU.mult))
                    dve.sem_inc(E_(f"tail_{d}"), 1)
                if q:
                    for d in range(2):
                        t = tile_of(q, s, d)
                        got(dve, f"v{q}{s}{d}")
                        link(cp(buf[d][XT], heads_col(la[:, t, 4 * d:4 * d + 4])))
                        dve.sem_inc(E_(f"spread_q_{d}"), 1)
                    for d in range(2):
                        t = tile_of(q, s, d)
                        dve.wait_ge(E_(f"gq_exp_{d}"), s + 1)
                        link(tt(buf[d][AT], buf[d][AT], gqT[:, :, (t - 2) * P:(t - 1) * P], ALU.mult))
                        dve.sem_inc(E_(f"queries_{d}"), 1)
                    for d in range(2):
                        t = tile_of(q, s, d)
                        got(dve, f"o{q}{s}{d}")
                        o = o_gdn[:, t - 2, :, :]
                        if s == 0:
                            link(cp(o, bank2(f"o{q}{s}{d}", 4)))
                        else:
                            link(tt(o, o, bank2(f"o{q}{s}{d}", 4), ALU.add))
                        read(dve, f"o{q}{s}{d}")
                for d in range(2):
                    name = f"S{q}{s}{d}"
                    got(dve, name)
                    for h in range(4):
                        z = stt(state[d][:, h, :], state[d][:, h, :], eglast[d][:, h:h + 1], bank2(name)[:, h * P:(h + 1) * P], ALU.mult, ALU.add)
                    link(z)
                    read(dve, name)

            for n, o in enumerate((o_ret, o_gdn)):
                o3 = o.rearrange("p t h d -> p (t h) d")
                q3 = oh.rearrange("p t h d -> p (t h) d")
                col = lambda a: a.rearrange("p (g o) -> p g o", o=1).broadcast_to([P, 8, C])
                if n == 0:
                    link(red(r8b, o3, AX.X, ALU.add))
                    link(ts(r8b, r8b, 1.0 / C, None, ALU.mult))
                    link(tt(o3, o3, col(r8b), ALU.subtract))
                link(tt(q3, o3, o3, ALU.mult))
                link(red(r8, q3, AX.X, ALU.add))
                link(ts(r8, r8, 1.0 / C, EPS, ALU.mult, ALU.add))
                nc.vector.reciprocal(r8, r8).then_inc(E_("mean_squares"), 1)
                dve.wait_ge(E_("roots"), n + 9)
                link(tt(o3, o3, col(r8), ALU.mult))
                dve.sem_inc(E_("heads_normed"), 1)
            dve.wait_ge(E_("gates_ready_2"), 1)
            for nm, dst, g, z_ in (("ryT", ryT, "ret_gn", rgT), ("gyT", gyT, "gdn_norm", gzT)):
                for t in range(2):
                    got(dve, f"{nm}{t}")
                    for k in range(4):
                        z = stt(dst[:, k, t * P:(t + 1) * P], bank2(f"{nm}{t}")[:, k * P:(k + 1) * P], V_(g, k), z_[:, k, t * P:(t + 1) * P], ALU.mult, ALU.mult)
                    link(z)
                    read(dve, f"{nm}{t}")
                dve.sem_inc(E_("branch_inputs"), 1)
            dve.wait_ge(E_("gates_ready_2"), 2)
            for n, nm in enumerate(("wr", "wg")):
                for i in range(4):
                    name = f"{nm}{i}"
                    g = gates2[:, 8 * n + 2 * i:8 * n + 2 * i + 2, :]
                    m = merged2[:, 2 * i:2 * i + 2, :]
                    got(dve, name)
                    link(stt(m if n == 0 else g, g, 1.0, bank2(name, 2), ALU.add, ALU.mult))
                    read(dve, name)
                    if n:
                        link(tt(m, m, g, ALU.add))
            dve.sem_inc(E_("merged2"), 1)
            for i in range(4):
                got(dve, f"wo{i}")
                link(ts(mo[:, 2 * i:2 * i + 2, :], bank2(f"wo{i}", 2), 0.5, None, ALU.mult))
                read(dve, f"wo{i}")
            dve.sem_inc(E_("x_steps"), 1)
            got(dve, "mnorm")
            inv(stat3[:, 0:T], bank2("mnorm")[:, 0:T], D)
            read(dve, "mnorm")
            nc.vector.reciprocal(stat3[:, 0:T], stat3[:, 0:T]).then_inc(E_("mean_squares"), 1)
            dve.wait_ge(E_("roots"), 11)
            link(tt(mo, mo, heads_row(stat3[:, 0:T], KT), ALU.mult))
            for k in range(KT):
                z = stt(xT[:, k, :], mo[:, k, :], gpost[:, k:k + 1], xT[:, k, :], ALU.mult, ALU.add)
            link(z)
            dve.sem_inc(E_("x_steps"), 1)
            got(dve, "fnorm")
            inv(stat3[:, 0:T], bank2("fnorm")[:, 0:T], D)
            read(dve, "fnorm")
            nc.vector.reciprocal(stat3[:, 0:T], stat3[:, 0:T]).then_inc(E_("mean_squares"), 1)
            dve.wait_ge(E_("roots"), 12)
            link(tt(h2T, xT[:, :, :], heads_row(stat3[:, 0:T], KT), ALU.mult))
            dve.sem_inc(E_("normed"), 1)
            dve.wait_ge(E_("split_h2"), 1)
            tt(h2_lo[:, :, :], h2T, h2_hi[:, :, :].bitcast(F32), ALU.subtract).then_inc(E_("split_h2"), 1)
            nc.vector.memset(zero, 0.0)
            dve.wait_ge(E_("router_exp"), 1)
            sc, bi, wt = rw[:, 0, :, :], rw[:, 1, :, :], rw[:, 2, :, :]
            link(ts(sc, sc, 1.0, None, ALU.add))
            link(nc.vector.reciprocal(sc, sc))
            rb = vec[:, VP["router_bias"]:VP["router_bias"] + 64].rearrange("p (o e) -> p o e", o=1).broadcast_to([P, 2, 64])
            link(tt(bi, sc, rb, ALU.add))
            for t in range(2):
                for g in range(8):
                    z = nc.vector.max(rw[:, 3 + t, g // 8, 8 * g:8 * g + 8], bi[:, t, 8 * g:8 * g + 8])
            link(z)
            for t in range(2):
                top = rw[:, 3 + t, 0, :].rearrange("p (g r) -> p g r", r=8)
                gs, m8, keep = rw[:, 5, t, 0:8], rw[:, 5, t, 8:16], rw[:, 5, t, 16:24]
                link(tt(gs, top[:, :, 0], top[:, :, 1], ALU.add))
                link(nc.vector.max(m8, gs))
                link(ts(keep, gs, m8[:, 3:4], None, ALU.is_ge))
                link(ts(keep, keep, -1.0, 1e30, ALU.add, ALU.mult))
                cand = rw[:, 6, t, :]
                link(tt(cand.rearrange("p (g r) -> p g r", r=8), bi[:, t, :].rearrange("p (g r) -> p g r", r=8),
                        keep.rearrange("p (g o) -> p g o", o=1).broadcast_to([P, 8, 8]), ALU.add))
                link(nc.vector.max(m8, cand))
                link(stt(wt[:, t, :], cand, m8[:, 7:8], sc[:, t, :], ALU.is_ge, ALU.mult))
                ssum = rw[:, 5, t, 32:33]
                link(red(ssum, wt[:, t, :], AX.X, ALU.add))
                link(nc.vector.reciprocal(ssum, ssum))
                link(ts(wt[:, t, :], wt[:, t, :], ssum, ROUTED_SCALE, ALU.mult, ALU.mult))
            dve.sem_inc(E_("routing_ready"), 1)
            got(dve, "wT")
            link(cp(wT_sb[0:64, :], ps[0:64, b2("wT"), 0:T]))
            read(dve, "wT")
            link(nc.vector.memset(wT_sb[64:65, :], 1.0))
            dve.sem_inc(E_("rows_ready_2"), 1)

            def hidden_of(s, count):
                dve.wait_ge(E_(f"silu_{s}"), count + 2)
                dve.wait_ge(E_(f"row_landed_{s}"), (count + 1) * 16)
                dve.wait_ge(E_(f"down_done_{s}"), count + 1)
                h = hid[:, s, :, :]
                link(tt(h, silu_g[:, s, :, :], ps[:, 2 * s + 1, :].rearrange("p (a t) -> p a t", a=2), ALU.mult))
                link(tt(h, h, wrow[:, s, :].rearrange("p (o t) -> p o t", o=1).broadcast_to([P, 2, T]), ALU.mult))
                link(cp(hid_hi[:, s, :, :], h))
                link(tt(hid_lo[:, s, :, :], h, hid_hi[:, s, :, :].bitcast(F32), ALU.subtract))
                dve.sem_inc(E_(f"hidden_{s}"), 1)

            def rest_gu(s, count):
                for n in range(2):
                    o = slice(2048 * n, 2048 * n + 2048)
                    dve.wait_ge(E_("gate_up_rounded"), count * 4 + 2 * s + n + 1)
                    z = tt(gu_lo[:, s, o], gu_mem[:, s, o], gu_hi[:, s, o].bitcast(F32), ALU.subtract)
                z.then_inc(E_("gate_up_rest"), 1)

            def rest_dn(s, count):
                dve.wait_ge(E_("down_rounded"), count * 2 + s + 1)
                tt(dn_lo[:, s, :], dn_mem[:, s, :], dn_hi[:, s, :].bitcast(F32), ALU.subtract).then_inc(E_("down_rest"), 1)

            link.restart()
            rest_gu(0, 0)
            with dve.Fori(0, EXPERTS // 2) as j:
                rest_gu(1, j)
                rest_dn(0, j)
                hidden_of(0, j)
                rest_gu(0, j + 1)
                rest_dn(1, j)
                hidden_of(1, j)
                link.restart()
            rest_dn(0, EXPERTS // 2)
            hidden_of(0, EXPERTS // 2)
            dve.wait_ge(E_("down_done_0"), EXPERTS // 2 + 2)
            dve.wait_ge(E_("down_done_1"), EXPERTS // 2 + 1)
            for b in range(4):
                z = cp(ymoe[:, 2 * b:2 * b + 2, :], ps[:, 4 + b, :].rearrange("p (a t) -> p a t", a=2))
            link(z)
            dve.sem_inc(E_("x_steps"), 1)
            dve.wait_ge(E_("y_sum"), 1)
            link(ts(stat4, ps[:, 0, 0:T], 1.0 / D, EPS, ALU.mult, ALU.add))
            nc.vector.reciprocal(stat4, stat4).then_inc(E_("mean_squares"), 1)
            dve.wait_ge(E_("roots"), 13)
            link(tt(ymoe, ymoe, heads_row(stat4, KT), ALU.mult))
            for k in range(KT):
                z = stt(xT[:, k, :], ymoe[:, k, :], gpost2[:, k:k + 1], xT[:, k, :], ALU.mult, ALU.add)
            z.then_inc(E_("x_out"), 1)

        block = ctx.enter_context(nc.Block())

        @block.sync
        def _(sp):
            sp.dma_start(cst[:, :], consts[:, 0:CP_FIRST]).then_inc(s_load, 16)
            sp.dma_start(vec[:, :], params_once).then_inc(s_load, 16)
            sp.dma_start(pos_i[:, :], positions).then_inc(s_load, 16)
            sp.dma_start(lay_all[:, :, :], params_layer).then_inc(s_load, 16)
            sp.dma_start(xT[:, :, :], x_t).then_inc(s_load, 16)
            with sp.Fori(0, NCHUNK // SLOTS) as i:
                for s in range(SLOTS):
                    sp.wait_ge(used[s], i + 1)
                    sp.dma_start(ring[:, s, :], stream[bass.ds(i * SLOTS + s, 1)].rearrange("a p n -> p (a n)")).then_inc(landed[s], 16)
            for s in range(NCHUNK % SLOTS):
                sp.wait_ge(used[s], NCHUNK // SLOTS + 1)
                sp.dma_start(ring[:, s, :], stream[NCHUNK // SLOTS * SLOTS + s]).then_inc(landed[s], 16)
            sync_tail(sp)

        @block.tensor
        def _(pe):
            ones_m = ones[:, :]
            for s_ in (*used, *free):
                pe.sem_inc(s_, 1)
            pe.wait_ge(s_csil, 1)
            for f in range(48):
                c, o = divmod(f * KT * P, CHUNK)
                if o == 0:
                    pe.wait_ge(landed[c % SLOTS], 16 * (c // SLOTS + 1))
                for k in range(KT):
                    mm = nc.tensor.matmul(ps[:, 7, 2 * f:2 * f + 2], ring[:, c % SLOTS, o + k * P:o + (k + 1) * P],
                                          csil[:, k, :], start=(k == 0), stop=(k == KT - 1))
                if f == 47:
                    mm.then_inc(s_mod, 1)
                elif (o + KT * P) == CHUNK:
                    mm.then_inc(used[c % SLOTS], 1)

            pending = [SLOTS - 1]

            def mul(o, lhs, rhs, start, stop):
                mm = nc.tensor.matmul(o, lhs, rhs, start=start, stop=stop)
                if pending and start and not stop:
                    mm.then_inc(used[pending.pop()], 1)
                return mm

            def spent(chunk):
                assert not pending
                pending.append(chunk % SLOTS)

            pe.wait_ge(s_load, 16 * 5)
            with pe.Fori(0, LAYERS) as l:
                def tiles(name, chunk, offset, lhs_cols, rhs, nk, half, rows=slice(0, P)):
                    for k in range(nk):
                        o = offset + k * lhs_cols
                        mm = mul(pair(name)[rows, half, :], ring[:, chunk % SLOTS, o:o + lhs_cols], rhs(k), k == 0, k == nk - 1)
                    return mm

                def done(mm, name, chunk=None):
                    mm.then_inc(full[bank_of(name)], 1)

                h = lambda k: hx[:, k, :]

                pe.wait_ge(s_sq, at(l, 2, 1))
                wait_free(pe, "x_norm", l)
                for k in range(KT):
                    mm = mul(pair("x_norm")[:, 0, :], ones_m, sq[:, k, :], k == 0, k == KT - 1)
                done(mm, "x_norm")

                pe.wait_ge(s_h, at(l, 2, 1))
                wait_chunk(pe, l, 0)
                for i in range(2):
                    wait_free(pe, f"q{i}", l)
                    for j in range(2):
                        mm = tiles(f"q{i}", 0, (2 * i + j) * 1024, P, h, KT, j)
                    done(mm, f"q{i}")
                spent(0)
                wait_chunk(pe, l, 1)
                wait_free(pe, "kv", l)
                tiles("kv", 1, 0, P, h, KT, 0)
                for t in range(2):
                    for k in range(KT):
                        mm = nc.tensor.matmul(pair("kv")[:, 1, t * P:(t + 1) * P], hx[:, k, t * P:(t + 1) * P],
                                              ring[:, 1, 1024 + k * P:1024 + (k + 1) * P], start=(k == 0), stop=(k == KT - 1))
                done(mm, "kv")
                wait_free(pe, "cq", l)
                tiles("cq", 1, 2048, P, h, KT, 0)
                done(tiles("cq", 1, 3072, P, h, KT, 1), "cq")
                spent(1)
                wait_chunk(pe, l, 2)
                wait_free(pe, "ckv", l)
                tiles("ckv", 2, 0, P, h, KT, 0)
                done(tiles("ckv", 2, 1024, 32, h, KT, 1, slice(64, 96)), "ckv")
                for i in range(4):
                    c = 3 + i // 2
                    if i % 2 == 0:
                        wait_chunk(pe, l, c)
                    wait_free(pe, f"u{i}", l)
                    tiles(f"u{i}", c, (i % 2) * 2048, P, h, KT, 0)
                    done(tiles(f"u{i}", c, (i % 2) * 2048 + 1024, P, h, KT, 1), f"u{i}")
                    if i % 2 == 1:
                        spent(c)
                pe.wait_ge(s_cq, at(l, 3, 2))
                wait_free(pe, "c_norm", l)
                for k in range(2):
                    nc.tensor.matmul(pair("c_norm")[:, 0, :], ones_m, csq[:, k, :], start=(k == 0), stop=(k == 1))
                done(nc.tensor.matmul(pair("c_norm")[:, 1, :], ones_m, csq[:, 2, :], start=True, stop=True), "c_norm")
                pe.wait_ge(s_cn, at(l, 1, 1))
                for i in range(4):
                    wait_free(pe, f"qup{i}", l)
                    for j in range(2):
                        mm = tiles(f"qup{i}", 2, 1280 + (2 * i + j) * 192, 96, lambda k: cqT[:, k, :], 2, j, slice(0, 96))
                    done(mm, f"qup{i}")
                for i in range(4):
                    wait_free(pe, f"kup{i}", l)
                    for j in range(2):
                        mm = tiles(f"kup{i}", 2, 2816 + (2 * i + j) * 64, 64, lambda k: ckvT[:, 0, :], 1, j, slice(0, 64))
                    done(mm, f"kup{i}")
                for t in range(2):
                    wait_free(pe, f"vup{t}", l)
                    done(nc.tensor.matmul(ps[:, bank_of(f"vup{t}"), :], ckvT[:, 0, t * P:(t + 1) * P],
                                          ring[:, 2, 3328:3840], start=True, stop=True), f"vup{t}")
                spent(2)

                def scores(n):
                    hd = n % HEADS
                    if n < 8:
                        b = 64 * (hd // 4)
                        q, k = qT[b:b + 64, hd % 4, :], kv[b:b + 64, 0, :]
                    else:
                        q, k = qcat[0:96, hd, :], kcat[0:96, hd, :]
                    if n == 0:
                        pe.wait_ge(s_qk, at(l, 3, 3))
                    if n == 8:
                        pe.wait_ge(s_rot, at(l, 1, 1))
                        pe.wait_ge(s_up, at(l, 10, 10))
                    if n >= 2:
                        pe.wait_ge(s_sm, at(l, 16, n - 1))
                    for t, (a, e) in enumerate(SEG):
                        mm = nc.tensor.matmul(ps[:, S_BANK + n % 2, a:e], q[:, t * P:(t + 1) * P], k[:, 0:e - a], start=True, stop=True)
                    mm.then_inc(s_sf, 1)

                def turn(n):
                    pe.wait_ge(s_pn, at(l, 16, n + 1))
                    if n >= 2:
                        pe.wait_ge(s_pt, at(l, 16, n - 1))
                    for s in range(3):
                        mm = nc.tensor.transpose(ps[:, T_BANK + n % 2, s * P:(s + 1) * P], probs[:, n % 3, s * P:(s + 1) * P], T_("ident", P))
                    mm.then_inc(s_tf, 1)

                def weigh(n):
                    hd = n % HEADS
                    pe.wait_ge(s_pt, at(l, 16, n + 1))
                    if n >= 4 and n % 2 == 0:
                        pe.wait_ge(s_y, at(l, 8, n // 2 - 1))
                    b = 64 * (hd % 2)
                    y = ps[b:b + 64, Y_BANK + (n // 2) % 2, 0:T]
                    v = (lambda t: kv[:, 1, t * P + 64 * (hd // 4):t * P + 64 * (hd // 4) + 64]) if n < 8 else (
                        lambda t: vm[:, t, hd * 64:(hd + 1) * 64])
                    nc.tensor.matmul(y[:, 0:P], v(0), pT[:, n % 2, 0:P], start=True, stop=True)
                    nc.tensor.matmul(y[:, P:T], v(0), pT[:, n % 2, P:2 * P], start=True, stop=False)
                    mm = nc.tensor.matmul(y[:, P:T], v(1), pT[:, n % 2, 2 * P:3 * P], start=False, stop=True)
                    mm.then_inc(s_pv, 1)

                half_at = [0]

                def gate_half():
                    g = half_at[0]
                    half_at[0] += 1
                    if g >= 24:
                        return
                    name, c = f"gate{g // 2}", 5 + g // 4
                    if g % 4 == 0:
                        wait_chunk(pe, l, c)
                    if g % 2 == 0:
                        wait_free(pe, name, l)
                    mm = tiles(name, c, (g % 4) * 1024, P, h, KT, g % 2)
                    if g % 2 == 1:
                        done(mm, name)
                    if g % 4 == 3:
                        spent(c)

                for i in range(19):
                    if i < 16:
                        scores(i)
                    gate_half()
                    if 2 <= i < 18:
                        turn(i - 2)
                    if i >= 3:
                        weigh(i - 3)
                gate_half()
                pe.wait_ge(s_cv, at(l, 1, 1))
                wait_free(pe, "conv_mean", l)
                for k in range(4):
                    mm = mul(pair("conv_mean")[:, 0, :], ones_m, conv[:, k, :], k == 0, k == 3)
                done(mm, "conv_mean")
                gate_half()
                gate_half()
                pe.wait_ge(s_cc, at(l, 1, 1))
                wait_free(pe, "conv_var", l)
                for k in range(4):
                    mm = mul(pair("conv_var")[:, 0, :], ones_m, upad[:, k, 0:T], k == 0, k == 3)
                done(mm, "conv_var")
                gate_half()
                gate_half()

                for b in range(3):
                    n = (0, 2, 1)[b]
                    if b == 0:
                        pe.wait_ge(s_y, at(l, 8, 8))
                    if b == 2:
                        pe.wait_ge(s_yc, at(l, 1, 1))
                    wait_chunk(pe, l, 11 + b)
                    for i in range(4):
                        name = f"branch{4 * b + i}"
                        wait_free(pe, name, l)
                        for j in range(2):
                            mm = tiles(name, 11 + b, (2 * i + j) * 512, P, lambda k: yT[:, 4 * n + k, :], 4, j)
                        done(mm, name)
                    spent(11 + b)
                pe.wait_ge(s_mg, at(l, 1, 1))
                for i in range(4):
                    c = 14 + i // 2
                    if i % 2 == 0:
                        wait_chunk(pe, l, c)
                    wait_free(pe, f"out{i}", l)
                    for j in range(2):
                        mm = tiles(f"out{i}", c, (i % 2 * 2 + j) * 1024, P, lambda k: merged[:, k, :], KT, j)
                    done(mm, f"out{i}")
                    if i % 2 == 1:
                        spent(c)
                pe.wait_ge(s_sq, at(l, 2, 2))
                wait_free(pe, "mlp_norm", l)
                for k in range(KT):
                    mm = mul(pair("mlp_norm")[:, 0, :], ones_m, sq[:, k, :], k == 0, k == KT - 1)
                done(mm, "mlp_norm")
                pe.wait_ge(s_h, at(l, 2, 2))
                for i in range(16):
                    c = 16 + i // 2
                    if i % 2 == 0:
                        wait_chunk(pe, l, c)
                    wait_free(pe, f"up{i}", l)
                    for j in range(2):
                        mm = tiles(f"up{i}", c, (i % 2 * 2 + j) * 1024, P, h, KT, j)
                    done(mm, f"up{i}")
                    if i % 2 == 1:
                        spent(c)
                for i in range(4):
                    wait_free(pe, f"down{i}", l)
                    for j in range(2):
                        c = 24 + 2 * i + j
                        wait_chunk(pe, l, c)
                        if i == 0 and j == 0:
                            pe.wait_ge(s_hd, at(l, 16, 16))
                        mm = tiles(f"down{i}", c, 0, P, lambda k: hidden[:, k, :], FF_TILES, j)
                        if j == 1:
                            done(mm, f"down{i}")
                        spent(c)
            second_tensor(pe)

        def gate_conv(act, l):
            act.wait_ge(s_cv, at(l, 1, 1))
            act.wait_ge(s_cl, at(l, 2, 1))
            nc.scalar.activation(upad[:, :, 0:T], conv[:, :, :], ACT.Square).then_inc(s_cc, 1)

        def gate_conv_var(act, l):
            act.wait_ge(s_var, at(l, 4, 3))
            nc.scalar.activation(stat[:, 0, :], stat[:, 0, :], ACT.Sqrt).then_inc(s_std, 1)
            act.wait_ge(s_cl, at(l, 2, 2))
            for k in range(4):
                mm = nc.scalar.activation(yT[:, 4 + k, :], conv[:, k, :], ACT.Silu, bias=L_("b_ln", k), scale=L_("g_ln", k))
            mm.then_inc(s_yc, 1)

        @block.scalar
        def _(act):
            link = Step(act, a_chain)
            act.wait_ge(s_load, 16 * 5)
            nc.scalar.activation(csil[:, :, 0], vec[:, VP["c"]:VP["c"] + 8], ACT.Exp, scale=-1.0)
            nc.scalar.activation(csil[:, :, 1], vec[:, VP["c_ctx"]:VP["c_ctx"] + 8], ACT.Exp, scale=-1.0).then_inc(s_sil, 1)
            act.wait_ge(s_ang, 1)
            nc.scalar.activation(rope_cs[64:96, 0, :], turns[64:96, 0, :], ACT.Sin)
            nc.scalar.activation(rope_cs[64:96, 1, :], turns[64:96, 1, :], ACT.Sin,
                                 scale=cst[64:96, CP["rope_sign"]:CP["rope_sign"] + 1]).then_inc(s_sin, 1)
            act.wait_ge(s_sin, 1)
            with act.Fori(0, LAYERS) as l:
                act.wait_ge(s_ld, at(l, 1, 1))
                nc.scalar.activation(sq[:, :, :], xT[:, :, :], ACT.Square).then_inc(s_sq, 1)
                act.wait_ge(s_var, at(l, 4, 1))
                nc.scalar.activation(stat[:, 0, :], stat[:, 0, :], ACT.Sqrt).then_inc(s_std, 1)
                for i in range(2):
                    wait_full(act, f"q{i}", l)
                    nc.scalar.copy(qT[:, 2 * i:2 * i + 2, :], pair(f"q{i}")).then_inc(free[bank_of(f"q{i}")], 1)
                wait_full(act, "kv", l)
                nc.scalar.copy(kv[:, :, :], pair("kv")).then_inc(free[bank_of("kv")], 1)
                wait_read(act, "kv", l)
                wait_read(act, "q1", l)
                act.sem_inc(s_qk, 3)
                wait_full(act, "cq", l)
                nc.scalar.activation(csq[:, 0:2, :], pair("cq"), ACT.Square).then_inc(s_cq, 1)
                nc.scalar.copy(cqT[:, :, :], pair("cq")).then_inc(free[bank_of("cq")], 1)
                wait_full(act, "ckv", l)
                nc.scalar.activation(csq[:, 2, :], pair("ckv")[:, 0, :], ACT.Square).then_inc(s_cq, 1)
                nc.scalar.copy(ckvT[:, 0, :], pair("ckv")[:, 0, :])
                link(nc.scalar.copy(ckvT[64:96, 1, :], pair("ckv")[64:96, 1, :]))
                act.sem_inc(free[bank_of("ckv")], 1)
                act.sem_inc(s_cq, 1)
                for i in range(4):
                    wait_full(act, f"u{i}", l)
                    if i >= 2:
                        wait_read(act, f"u{i - 2}", l)
                    nc.scalar.activation(tanh_g[:, i % 2, :], pair(f"u{i}")[:, 1, :], ACT.Tanh, scale=0.5).then_inc(s_tg, 1)
                act.wait_ge(s_var, at(l, 4, 2))
                nc.scalar.activation(stat[:, :, :], stat[:, :, :], ACT.Sqrt).then_inc(s_std, 1)
                for i in range(4):
                    wait_full(act, f"qup{i}", l)
                    link(nc.scalar.copy(qcat[0:96, 2 * i:2 * i + 2, :], pair(f"qup{i}")[0:96]))
                    act.sem_inc(free[bank_of(f"qup{i}")], 1)
                    act.sem_inc(s_up, 1)
                for i in range(4):
                    wait_full(act, f"kup{i}", l)
                    link(nc.scalar.copy(kcat[0:64, 2 * i:2 * i + 2, :], pair(f"kup{i}")[0:64]))
                    act.sem_inc(free[bank_of(f"kup{i}")], 1)
                    act.sem_inc(s_up, 1)
                for t in range(2):
                    wait_full(act, f"vup{t}", l)
                    link(nc.scalar.copy(vm[:, t, :], ps[:, bank_of(f"vup{t}"), :]))
                    act.sem_inc(free[bank_of(f"vup{t}")], 1)
                    act.sem_inc(s_up, 1)

                gate_at = [0]

                def gate_tanh():
                    g = gate_at[0]
                    gate_at[0] += 1
                    wait_full(act, f"gate{g}", l)
                    if g == 11:
                        nc.scalar.activation(gates[:, 2 * g:2 * g + 2, :], pair(f"gate{g}"), ACT.Tanh, scale=0.5).then_inc(free[bank_of(f"gate{g}")], 1)
                    else:
                        nc.scalar.activation(gates[:, 2 * g:2 * g + 2, :], pair(f"gate{g}"), ACT.Tanh, scale=0.5).then_inc(free[bank_of(f"gate{g}")], 1)

                def exps(n):
                    act.wait_ge(s_nm, at(l, 16, n + 1))
                    for t, (a, e) in enumerate(SEG):
                        mm = nc.scalar.activation(probs[:, n % 3, a:e], probs[:, n % 3, a:e], ACT.Exp,
                                                  bias=nmax[:, n % 3, t:t + 1], accum_out=esum[:, n % 3, t:t + 1])
                    if n < 8:
                        mm = nc.scalar.activation(nmax[:, n % 3, 2:4], nmax[:, n % 3, 0:2], ACT.Exp, bias=L_("sinks", n))
                    mm.then_inc(s_ex, 1)

                def copy_turned(n):
                    act.wait_ge(s_tf, at(l, 16, n + 1))
                    if n >= 2:
                        act.wait_ge(s_pv, at(l, 16, n - 1))
                    nc.scalar.copy(pT[:, n % 2, :], ps[:, T_BANK + n % 2, 0:384]).then_inc(s_pt, 1)

                def copy_y(m):
                    act.wait_ge(s_pv, at(l, 16, 2 * m + 2))
                    y = m if m < 4 else 4 + m
                    nc.scalar.copy(yT[:, y, :], ps[:, Y_BANK + m % 2, 0:T]).then_inc(s_y, 1)

                for i in range(19):
                    if i < 16:
                        exps(i)
                    if i % 2 == 1:
                        gate_tanh()
                    if 2 <= i < 18:
                        copy_turned(i - 2)
                    if i >= 4 and i % 2 == 0:
                        copy_y((i - 4) // 2)
                gate_tanh()
                gate_conv(act, l)
                gate_tanh()
                gate_conv_var(act, l)
                gate_tanh()
                act.wait_ge(s_xo, at(l, 1, 1))
                act.wait_ge(s_mg, at(l, 1, 1))
                nc.scalar.activation(sq[:, :, :], xT[:, :, :], ACT.Square).then_inc(s_sq, 1)
                act.wait_ge(s_var, at(l, 4, 4))
                nc.scalar.activation(stat[:, 0, :], stat[:, 0, :], ACT.Sqrt).then_inc(s_std, 1)
                for i in range(16):
                    wait_full(act, f"up{i}", l)
                    if i >= 2:
                        act.wait_ge(s_hd, at(l, 16, i - 1))
                    nc.scalar.activation(relu[:, i % 2, :], ps[:, bank_of(f"up{i}"), :], ACT.Relu).then_inc(free[bank_of(f"up{i}")], 1)
                link.restart()
            second_scalar(act)

        @block.vector
        def _(dve):
            link = Step(dve, v_chain)
            tt, ts, stt = nc.vector.tensor_tensor, nc.vector.tensor_scalar, nc.vector.scalar_tensor_tensor
            nc.vector.memset(ones[:, :], 1.0)
            for k in range(4):
                z = nc.vector.memset(upad[:, k, 0:CONV_W - 1], 0.0)
            link(z)
            dve.wait_ge(s_load, 16 * 5)
            dve.wait_ge(s_sil, 1)
            link(ts(csil[:, :, :], csil[:, :, :], 1.0, None, ALU.add))
            link(nc.vector.reciprocal(csil[:, :, :], csil[:, :, :]))
            link(tt(csil[:, :, 0], csil[:, :, 0], vec[:, VP["c"]:VP["c"] + 8], ALU.mult))
            tt(csil[:, :, 1], csil[:, :, 1], vec[:, VP["c_ctx"]:VP["c_ctx"] + 8], ALU.mult).then_inc(s_csil, 1)
            link(nc.vector.tensor_copy(pos_f[:, :], pos_i[:, :]))
            for t, (a, e) in enumerate(SEG):
                z = ts(dist[:, a:e], pos_f[:, 0:e - a], pos_f[:, T + t:T + t + 1], -1.0, ALU.subtract, ALU.mult)
            rel0 = VP["rel_bias"]
            tt(delta[:, 8:256], vec[:, rel0 + 8:rel0 + 256], vec[:, rel0:rel0 + 248], ALU.subtract)
            freq = cst[64:96, CP["rope_freq"]:CP["rope_freq"] + 1]
            A = turns[64:96, 2, :]
            link(ts(A, pos_f[64:96, 0:T], freq, None, ALU.mult))
            two_pi = 2 * np.pi
            c1 = 6.28125
            c2 = float(np.float32(0.0019350051879882812))
            c3 = float(two_pi - c1 - c2)
            for n in range(2):
                R = turns[64:96, n, :]
                link(ts(R, A, 1.0 / two_pi, 0.25 if n == 0 else 0.0, ALU.mult, ALU.add))
                link(nc.vector.tensor_copy(turns_i[64:96, :], R))
                K = tanh_g[64:96, n, :]
                link(nc.vector.tensor_copy(K, turns_i[64:96, :]))
                link(stt(R, K, -c1, A, ALU.mult, ALU.add))
                link(stt(R, K, -c2, R, ALU.mult, ALU.add))
                link(stt(R, K, -c3, R, ALU.mult, ALU.add))
                if n == 0:
                    link(ts(R, R, float(np.pi / 2), None, ALU.add))
                z = ts(R, R, 3.1415925, -3.1415925, ALU.min, ALU.max)
                if n == 0:
                    link(z)
            z.then_inc(s_ang, 1)
            for hd in range(HEADS):
                z = ts(bias[:, hd, :], T_("band", 384), vec[:, rel0 + hd:rel0 + hd + 1], None, ALU.add)
            link(z)
            link.restart()
            with dve.Fori(1, N_BUCKETS) as b:
                link(ts(reached, dist, cst[:, bass.ds(b + CP["thr"], 1)], None, ALU.is_ge))
                for hd in range(HEADS):
                    z = stt(bias[:, hd, :], reached, delta[:, bass.ds(b * HEADS + hd, 1)], bias[:, hd, :], ALU.mult, ALU.add)
                link(z)
                link.restart()
            dve.wait_ge(s_mod, 1)
            b_mod = vec[:, VP["b_mod"]:VP["b_mod"] + 48]
            for n in range(2):
                z = tt(modT[:, :, n], ps[:, 7, 0:96].rearrange("p (f n) -> p f n", n=2)[:, :, n], b_mod, ALU.add)
            link(z)
            for n in (1, 4):
                z = ts(modT[:, 8 * n:8 * n + 8, :], modT[:, 8 * n:8 * n + 8, :], 1.0, None, ALU.add)
            link(z)
            dve.sem_inc(s_modT, 1)
            link.restart()

            with dve.Fori(0, LAYERS) as l:
                link(nc.vector.tensor_copy(lay[:, :], lay_all[:, bass.ds(l, 1), :].rearrange("p a n -> p (a n)")))
                dve.sem_inc(s_ld, 1)
                ts(half_w[:, :], lay[:, LP["w_dw"]:LP["w_dw"] + 4 * CONV_W], 0.5, None, ALU.mult)

                def norm(name, cols, n, dst, g_name, src):
                    wait_full(dve, name, l)
                    link(ts(stat[:, 0, :], pair(name)[:, 0, :], 1.0 / cols, EPS, ALU.mult, ALU.add))
                    dve.sem_inc(free[bank_of(name)], 1)
                    nc.vector.reciprocal(stat[:, 0, :], stat[:, 0, :]).then_inc(s_var, 1)
                    dve.wait_ge(s_std, at(l, 4, n))
                    for k in range(KT):
                        z = stt(dst[:, k, :], src[:, k, :], L_(g_name, k), stat[:, 0, :], ALU.mult, ALU.mult)
                    z.then_inc(s_h, 1)

                norm("x_norm", D, 1, hx, "g_mix", xT)
                for i in range(4):
                    dve.wait_ge(s_tg, at(l, 4, i + 1))
                    stt(upad[:, i, CONV_W - 1:], tanh_g[:, i % 2, :], 1.0, pair(f"u{i}")[:, 0, :], ALU.add, ALU.mult).then_inc(free[bank_of(f"u{i}")], 1)
                wait_full(dve, "c_norm", l)
                dve.wait_ge(s_cq, at(l, 3, 3))
                ts(stat[:, 0, :], pair("c_norm")[:, 0, :], 1.0 / 256, EPS, ALU.mult, ALU.add)
                link(ts(stat[:, 1, :], pair("c_norm")[:, 1, :], 1.0 / 128, EPS, ALU.mult, ALU.add))
                dve.sem_inc(free[bank_of("c_norm")], 1)
                nc.vector.reciprocal(stat[:, :, :], stat[:, :, :]).then_inc(s_var, 1)
                dve.wait_ge(s_std, at(l, 4, 2))
                for k in range(2):
                    stt(cqT[:, k, :], cqT[:, k, :], L_("g_q", k), stat[:, 0, :], ALU.mult, ALU.mult)
                stt(ckvT[:, 0, :], ckvT[:, 0, :], L_("g_kv", 0), stat[:, 1, :], ALU.mult, ALU.mult).then_inc(s_cn, 1)

                swap = [(i + 16) % 32 for i in range(32)]
                cos, sin = rope_cs[64:96, 0, :], rope_cs[64:96, 1, :]
                dve.wait_ge(s_sin, 1)

                def wide(a, n):
                    return a.rearrange("p (o t) -> p o t", o=1).broadcast_to([32, n, T])

                kr = ckvT[64:96, 1, :]
                r0 = rot[64:96, 0:T]
                link(tt(r0, kr, cos, ALU.mult))
                link(nc.vector.stream_shuffle(kr, kr, swap))
                link(tt(kr, kr, sin, ALU.mult))
                link(tt(kr, kr, r0, ALU.add))
                nc.vector.tensor_copy(kcat[64:96, :, :], wide(kr, HEADS))
                for g in range(2):
                    dve.wait_ge(s_up, at(l, 10, 2 * g + 2))
                    q = qcat[64:96, 4 * g:4 * g + 4, :]
                    r = rot[64:96, :].rearrange("p (h t) -> p h t", h=4)
                    link(tt(r, q, wide(cos, 4), ALU.mult))
                    link(nc.vector.stream_shuffle(q, q, swap))
                    link(tt(q, q, wide(sin, 4), ALU.mult))
                    link(tt(q, q, r, ALU.add))
                dve.sem_inc(s_rot, 1)

                taps = [(k, w) for w in range(CONV_W) for k in range(4)]
                tap_at = [0]

                def conv_steps(n):
                    for k, w in taps[tap_at[0]:tap_at[0] + n]:
                        u = upad[:, k, w:w + T]
                        tap = half_w[:, k * CONV_W + w:k * CONV_W + w + 1]
                        if w == 0:
                            z = ts(conv[:, k, :], u, tap, L_("b_dw", k), ALU.mult, ALU.add)
                        else:
                            z = stt(conv[:, k, :], u, tap, conv[:, k, :], ALU.mult, ALU.add)
                        if k == 3:
                            link(z)
                        tap_at[0] += 1

                def soften(n):
                    hd = n % HEADS
                    dve.wait_ge(s_sf, at(l, 16, n + 1))
                    if n >= 3:
                        dve.wait_ge(s_tf, at(l, 16, n - 2))
                    m = bias[:, hd, :] if n < 8 else T_("causal", 384)
                    scale = 64 ** -0.5 if n < 8 else 96 ** -0.5
                    p_ = probs[:, n % 3, :]
                    link(stt(p_, ps[:, S_BANK + n % 2, 0:384], float(scale), m, ALU.mult, ALU.add))
                    dve.sem_inc(s_sm, 1)
                    for t, (a, e) in enumerate(SEG):
                        z = nc.vector.tensor_reduce(nmax[:, n % 3, t:t + 1], p_[:, a:e], AX.X, ALU.max)
                    link(z)
                    if n < 8:
                        ts(nmax[:, n % 3, 0:2], nmax[:, n % 3, 0:2], L_("sinks", n), -1.0, ALU.max, ALU.mult).then_inc(s_nm, 1)
                    else:
                        ts(nmax[:, n % 3, 0:2], nmax[:, n % 3, 0:2], -1.0, None, ALU.mult).then_inc(s_nm, 1)

                def normalise(n):
                    dve.wait_ge(s_ex, at(l, 16, n + 1))
                    e2 = esum[:, n % 3, 0:2]
                    if n < 8:
                        link(tt(e2, e2, nmax[:, n % 3, 2:4], ALU.add))
                    link(nc.vector.reciprocal(e2, e2))
                    for t, (a, e) in enumerate(SEG):
                        z = ts(probs[:, n % 3, a:e], probs[:, n % 3, a:e], esum[:, n % 3, t:t + 1], None, ALU.mult)
                    z.then_inc(s_pn, 1)

                for i in range(17):
                    if i < 16:
                        soften(i)
                    conv_steps(8)
                    if i >= 1:
                        normalise(i - 1)
                conv_steps(len(taps))
                dve.sem_inc(s_cv, 1)

                wait_full(dve, "conv_mean", l)
                link(ts(stat[:, 0, :], pair("conv_mean")[:, 0, :], 1.0 / 512, None, ALU.mult))
                dve.sem_inc(free[bank_of("conv_mean")], 1)
                for k in range(4):
                    z = tt(conv[:, k, :], conv[:, k, :], stat[:, 0, :], ALU.subtract)
                z.then_inc(s_cl, 1)
                wait_full(dve, "conv_var", l)
                link(ts(stat[:, 0, :], pair("conv_var")[:, 0, :], 1.0 / 512, EPS, ALU.mult, ALU.add))
                dve.sem_inc(free[bank_of("conv_var")], 1)
                nc.vector.reciprocal(stat[:, 0, :], stat[:, 0, :]).then_inc(s_var, 1)
                dve.wait_ge(s_std, at(l, 4, 3))
                for k in range(4):
                    z = tt(conv[:, k, :], conv[:, k, :], stat[:, 0, :], ALU.mult)
                z.then_inc(s_cl, 1)
                dve.wait_ge(s_std, at(l, 4, 3))
                nc.vector.memset(upad[:, :, 0:CONV_W - 1], 0.0)

                for b in range(3):
                    n = (0, 2, 1)[b]
                    for i in range(4):
                        name = f"branch{4 * b + i}"
                        wait_full(dve, name, l)
                        if b == 0 and i == 0:
                            wait_read(dve, "gate11", l)
                        g = gates[:, 8 * n + 2 * i:8 * n + 2 * i + 2, :]
                        if b == 0:
                            stt(merged[:, 2 * i:2 * i + 2, :], g, 1.0, pair(name), ALU.add, ALU.mult).then_inc(free[bank_of(name)], 1)
                        else:
                            stt(g, g, 1.0, pair(name), ALU.add, ALU.mult).then_inc(free[bank_of(name)], 1)
                            wait_read(dve, name, l)
                            z = tt(merged[:, 2 * i:2 * i + 2, :], merged[:, 2 * i:2 * i + 2, :], g, ALU.add)
                z.then_inc(s_mg, 1)
                for i in range(4):
                    wait_full(dve, f"out{i}", l)
                    xs = xT[:, 2 * i:2 * i + 2, :]
                    stt(xs, pair(f"out{i}"), 0.5, xs, ALU.mult, ALU.add).then_inc(free[bank_of(f"out{i}")], 1)
                for i in (2, 3):
                    wait_read(dve, f"out{i}", l)
                dve.sem_inc(s_xo, 1)
                norm("mlp_norm", D, 4, hx, "g_mlp", xT)
                for i in range(16):
                    wait_read(dve, f"up{i}", l)
                    r = relu[:, i % 2, :].rearrange("p (h t) -> p h t", h=2)
                    tt(hidden[:, 2 * i:2 * i + 2, :], r, r, ALU.mult).then_inc(s_hd, 1)
                for i in range(4):
                    wait_full(dve, f"down{i}", l)
                    xs = xT[:, 2 * i:2 * i + 2, :]
                    tt(xs, xs, pair(f"down{i}"), ALU.add).then_inc(free[bank_of(f"down{i}")], 1)
                for i in (2, 3):
                    wait_read(dve, f"down{i}", l)
                dve.sem_inc(s_end, 1)
                link.restart()
            second_vector(dve)


def _tiles(w, cols):
    k = w.shape[0] // P
    return w[:, cols].reshape(k, P, -1).transpose(1, 0, 2).reshape(P, -1)


def _chunks(parts):
    out, cur, n = [], [], 0
    for a in parts:
        if n + a.shape[1] > CHUNK:
            cur.append(np.zeros((P, CHUNK - n), np.float32))
            out.append(np.concatenate(cur, 1))
            cur, n = [], 0
        cur.append(a)
        n += a.shape[1]
    cur.append(np.zeros((P, CHUNK - n), np.float32))
    out.append(np.concatenate(cur, 1))
    return np.stack(out)


def _features(w, first, count, width=P):
    return [_tiles(w, np.arange(first + i * width, first + (i + 1) * width)) for i in range(count)]


def _layer_stream(w_in, w_q_up, w_kv_up, w_branch, w_out, w_up, w_down):
    r = np.arange
    parts = [_tiles(w_in, np.concatenate([r(64 * j, 64 * j + 64), r(64 * (j + 4), 64 * (j + 4) + 64)])) for j in range(4)]
    parts += _features(w_in, 512, 1) + _features(w_in, 640, 1) + _features(w_in, 1792, 2)
    c2 = _features(w_in, 2048, 1) + [_tiles(w_in, r(2176, 2208))]
    c2 += [_tiles(w_q_up, r(96 * h, 96 * h + 96)) for h in range(8)]
    c2 += [_tiles(w_kv_up, r(128 * h, 128 * h + 64)) for h in range(8)]
    c2 += [_tiles(w_kv_up, np.concatenate([r(128 * h + 64, 128 * h + 128) for h in range(8)]))]
    u = []
    for i in range(4):
        u += _features(w_in, 768 + 128 * i, 1) + _features(w_in, 1280 + 128 * i, 1)
    rest = _features(w_in, 2208, 24)
    for n in (0, 2, 1):
        rest += _features(w_branch[n], 0, 8)
    rest += _features(w_out, 0, 8) + _features(w_up, 0, 32) + _features(w_down, 0, 8)
    return np.concatenate([_chunks(parts), _chunks(c2), _chunks(u), _chunks(rest)])


def _mix_stream(w_in, w_ret, w_gdn, w_o):
    r = np.arange
    S = 2064
    parts = [_tiles(w_in, r(0, 512)), _tiles(w_in, r(512, 1024))]
    parts += _features(w_in, 1024, 8)
    rest = [_tiles(w_in, r(S, S + 512))]
    rest += _features(w_in, S + 1024, 4) + _features(w_in, S + 512, 4) + _features(w_in, S + 1536, 4)
    rest += _features(w_in, S + 2048, 16)
    rest += _features(w_ret, 0, 8) + _features(w_gdn, 0, 8) + _features(w_o, 0, 8)
    return np.concatenate([_chunks(parts), _chunks(rest)])


def _columns(v):
    return np.asarray(v).reshape(-1, P).T


def _everywhere(v):
    return np.tile(np.asarray(v).reshape(1, -1), (P, 1))


def arrays_of(i):
    a = {k: np.asarray(v) for k, v in i.items()}
    stream = [_chunks(_features(a["w_mod_2"][0], 0, 48))]
    for l in range(LAYERS):
        stream.append(_layer_stream(a["w_in"][l], a["w_q_up"][l], a["w_kv_up"][l], a["w_branch"][l], a["w_out"][l],
                                    a["w_up"][l], a["w_down"][l]))
    stream.append(_mix_stream(a["w_in_2"][0], a["w_ret_out_2"][0], a["w_gdn_out_2"][0], a["w_o_2"][0]))
    stream = np.concatenate(stream)
    assert stream.shape[0] == MOD_CHUNKS + LAYERS * LAYER_CHUNKS + MIX_CHUNKS, stream.shape
    gate = np.concatenate([a["w_gate_2"][0], a["w_sh_gate_2"]])
    up = np.concatenate([a["w_up_2"][0], a["w_sh_up_2"]])
    down = np.concatenate([a["w_down_2"][0], a["w_sh_down_2"]])
    n = EXPERTS + 1
    gu = np.stack([gate, up], 1).reshape(n, 2, 8, P, 2, P).transpose(0, 3, 1, 4, 2, 5).reshape(n, P, CHUNK)
    dn = down.reshape(n, 2, P, 8, P).transpose(0, 2, 3, 1, 4).reshape(n, P, 2048)
    experts = np.concatenate([gu, dn], 2)
    lay = np.zeros((P, LAYERS, LP_COLS), np.float32)
    for l in range(LAYERS):
        dw = a["w_dw"][l][:, 0, :].T.reshape(4, P, CONV_W).transpose(1, 0, 2).reshape(P, -1)
        lay[:, l, :] = np.concatenate([_columns(a["g_mix"][l]), _columns(a["g_mlp"][l]), _columns(a["g_q_norm"][l]),
                                       _columns(a["g_kv_norm"][l]), dw, _columns(a["b_dw"][l]),
                                       _columns(a["g_conv_ln"][l]), _columns(a["b_conv_ln"][l]),
                                       _everywhere(a["swa_sinks"][l])], 1)
    conv = a["gdn_conv_2"][0]
    conv = conv.T.reshape(12, P, 3).transpose(1, 0, 2).reshape(P, 36)
    vec = np.concatenate([_columns(a["g_final"]), _everywhere(a["rel_bias"]), _columns(a["c_2"][0]),
                          _columns(a["c_ctx_2"]), _columns(a["b_mod_2"][0]), _columns(a["norm_mix_pre_2"][0]),
                          _columns(a["norm_mix_post_2"][0]), _columns(a["norm_ffn_pre_2"][0]),
                          _columns(a["norm_ffn_post_2"][0]), conv, _columns(a["ret_gn_w_2"][0]),
                          _columns(a["gdn_norm_w_2"][0]), _everywhere(a["ret_log_decay_2"][0]),
                          _everywhere(a["gdn_a_log_2"][0]), _everywhere(a["gdn_dt_bias_2"][0]),
                          _everywhere(a["router_bias_2"][0])], 1)
    pos = a["positions"][0]
    pos = np.concatenate([_everywhere(pos), _columns(pos)], 1)
    return {"stream": stream, "experts": experts, "params_once": np.ascontiguousarray(vec), "params_layer": lay,
            "consts": tables(), "positions": pos, "ctx_t": _rows(a["ctx_2"][0]), "x_t": _rows(a["x"][0]),
            "small": np.concatenate([_tiles(a["w_in_2"][0], np.arange(2048, 2064)), _tiles(a["w_router_2"][0], np.arange(EXPERTS))], 1)}


def _rows(x):
    return np.ascontiguousarray(x.T.reshape(KT, P, -1).transpose(1, 0, 2))


def program(nc, arrays):
    ap = {k: nc.dram_tensor(f"in_{k}", v.shape, mybir.dt.from_np(v.dtype), kind="ExternalInput").ap()
          for k, v in arrays.items()}
    wt_rows = nc.dram_tensor("expert_weights", (EXPERTS + 1, T), F32, kind="Internal").ap()
    out = nc.dram_tensor("out_0", (P, KT, T), F32, kind="ExternalOutput").ap()
    build(nc, wt_rows=wt_rows, out=out, **ap)


def kernel(**inputs):
    import concourse.bacc as bacc
    from concourse.bass_utils import run_bass_kernel_spmd

    arrays = arrays_of(inputs)
    nc = bacc.Bacc("TRN2", target_bir_lowering=False, num_devices=1)
    program(nc, arrays)
    r = run_bass_kernel_spmd(nc, [{f"in_{k}": v for k, v in arrays.items()}], core_ids=[0])
    got = r.results[0]["out_0"]
    return np.ascontiguousarray(got.transpose(2, 1, 0).reshape(1, T, D))
```
